# Optimizing a Trainium2 kernel written in Bass

```python
import jax, jax.numpy as jnp
from jax import lax
import numpy as np

D_MODEL = 1024
BATCH = 1
SEQ = 1024
DEPTH = 2

CHUNK = 64
HEAD_DIM = 64
MIX_WIDTH = D_MODEL
SWA_Q_HEADS = MIX_WIDTH // (2 * HEAD_DIM)
SWA_KV_HEADS = SWA_Q_HEADS // 4
SWA_GROUP = SWA_Q_HEADS // SWA_KV_HEADS
SWA_WINDOW = 128
SWA_WINDOW_CHUNKS = SWA_WINDOW // CHUNK
FOX_HEADS = MIX_WIDTH // (2 * HEAD_DIM)
SWA_WIDTH = SWA_Q_HEADS * HEAD_DIM
SWA_KV_WIDTH = SWA_KV_HEADS * HEAD_DIM
FOX_WIDTH = FOX_HEADS * HEAD_DIM
ROPE_THETA = 10000.0
RMS_EPS = 1e-6
Q_BLOCK = 128
SPLIT_SIZES = (SWA_WIDTH, SWA_KV_WIDTH, SWA_KV_WIDTH, SWA_WIDTH,
               FOX_WIDTH, FOX_WIDTH, FOX_WIDTH, FOX_HEADS, FOX_WIDTH)
IN_WIDTH = SWA_WIDTH + 2 * SWA_KV_WIDTH + SWA_WIDTH + 3 * FOX_WIDTH + FOX_HEADS + FOX_WIDTH

kernel_name = "hybrid_swa_sink_fox_parallel_heads"

def rms_norm(x, g):
    xf = x.astype(jnp.float32)
    y = xf * lax.rsqrt(jnp.mean(xf * xf, axis=-1, keepdims=True) + RMS_EPS)
    return (y * g.astype(jnp.float32)).astype(x.dtype)

def rope(x, positions):
    half = HEAD_DIM // 2
    inv_freq = ROPE_THETA ** (-jnp.arange(0, half, dtype=jnp.float32) / half)
    ang = positions.astype(jnp.float32)[:, None] * inv_freq[None, :]
    cos = jnp.cos(ang)[None, :, None, :]
    sin = jnp.sin(ang)[None, :, None, :]
    xf = x.astype(jnp.float32)
    x1, x2 = xf[..., :half], xf[..., half:]
    out = jnp.concatenate([x1 * cos - x2 * sin, x2 * cos + x1 * sin], axis=-1)
    return out.astype(x.dtype)

def split_columns(proj):
    outs, start = [], 0
    for size in SPLIT_SIZES:
        outs.append(proj[..., start:start + size])
        start += size
    return outs

def swa_sink_attention(q, k, v, sinks):
    B, S = q.shape[0], q.shape[1]
    nb = S // Q_BLOCK
    qb = q.reshape(B, nb, Q_BLOCK, SWA_KV_HEADS, SWA_GROUP, HEAD_DIM)
    kb = k.reshape(B, nb, Q_BLOCK, SWA_KV_HEADS, HEAD_DIM)
    vb = v.reshape(B, nb, Q_BLOCK, SWA_KV_HEADS, HEAD_DIM)
    pad = ((0, 0), (1, 0), (0, 0), (0, 0), (0, 0))
    k_prev = jnp.pad(kb, pad)[:, :-1]
    v_prev = jnp.pad(vb, pad)[:, :-1]
    keys = jnp.concatenate([k_prev, kb], axis=2)
    vals = jnp.concatenate([v_prev, vb], axis=2)
    scale = HEAD_DIM ** -0.5
    s = jnp.einsum('bnqhgd,bnkhd->bnhgqk', qb, keys,
                   preferred_element_type=jnp.float32) * scale
    blk = jnp.arange(nb)[:, None, None]
    qpos = blk * Q_BLOCK + jnp.arange(Q_BLOCK)[None, :, None]
    kpos = (blk - 1) * Q_BLOCK + jnp.arange(2 * Q_BLOCK)[None, None, :]
    qc, kc = qpos // CHUNK, kpos // CHUNK
    allowed = (kpos >= 0) & (kc <= qc) & (kc > qc - SWA_WINDOW_CHUNKS)
    s = jnp.where(allowed[None, :, None, None], s, -jnp.inf)
    sink = sinks.astype(jnp.float32).reshape(SWA_KV_HEADS, SWA_GROUP)
    sink_col = jnp.broadcast_to(sink[None, None, :, :, None, None], s.shape[:-1] + (1,))
    p = jax.nn.softmax(jnp.concatenate([s, sink_col], axis=-1), axis=-1)[..., :-1]
    o = jnp.einsum('bnhgqk,bnkhd->bnqhgd', p.astype(vals.dtype), vals)
    return o.reshape(B, S, SWA_WIDTH)

def forgetting_attention(q, k, v, f_logit, b_f):
    B, S = q.shape[0], q.shape[1]
    nb = S // Q_BLOCK
    log_f = jax.nn.log_sigmoid(f_logit.astype(jnp.float32) + b_f.astype(jnp.float32))
    c = jnp.cumsum(log_f, axis=1).transpose(0, 2, 1)
    k_t = k.transpose(0, 2, 1, 3)
    v_t = v.transpose(0, 2, 1, 3)
    q_blocks = q.reshape(B, nb, Q_BLOCK, FOX_HEADS, HEAD_DIM).transpose(1, 0, 3, 2, 4)
    c_blocks = c.reshape(B, FOX_HEADS, nb, Q_BLOCK).transpose(2, 0, 1, 3)
    kpos = jnp.arange(S)
    scale = HEAD_DIM ** -0.5

    def block(args):
        qb, cqb, n = args
        s = jnp.einsum('bhqd,bhkd->bhqk', qb, k_t,
                       preferred_element_type=jnp.float32) * scale
        s = s + (cqb[..., :, None] - c[:, :, None, :])
        qpos = n * Q_BLOCK + jnp.arange(Q_BLOCK)
        s = jnp.where(kpos[None, :] <= qpos[:, None], s, -jnp.inf)
        p = jax.nn.softmax(s, axis=-1)
        return jnp.einsum('bhqk,bhkd->bhqd', p.astype(v_t.dtype), v_t)

    o = lax.map(block, (q_blocks, c_blocks, jnp.arange(nb)))
    return o.transpose(1, 0, 3, 2, 4).reshape(B, S, FOX_WIDTH)

def hybrid_layer(x, w_in, b_f, sinks, w_out, g_pre, g_post, positions):
    B, S = x.shape[0], x.shape[1]
    h = rms_norm(x, g_pre)
    proj = jnp.einsum('bsd,de->bse', h, w_in)
    q_a, k_a, v_a, gate_a, q_b, k_b, v_b, f_b, gate_b = split_columns(proj)
    q_a = rope(q_a.reshape(B, S, SWA_Q_HEADS, HEAD_DIM), positions)
    k_a = rope(k_a.reshape(B, S, SWA_KV_HEADS, HEAD_DIM), positions)
    v_a = v_a.reshape(B, S, SWA_KV_HEADS, HEAD_DIM)
    y_a = swa_sink_attention(q_a, k_a, v_a, sinks) * jax.nn.silu(gate_a)
    q_b = q_b.reshape(B, S, FOX_HEADS, HEAD_DIM)
    k_b = k_b.reshape(B, S, FOX_HEADS, HEAD_DIM)
    v_b = v_b.reshape(B, S, FOX_HEADS, HEAD_DIM)
    y_b = forgetting_attention(q_b, k_b, v_b, f_b, b_f) * jax.nn.silu(gate_b)
    y = jnp.einsum('bse,ed->bsd', jnp.concatenate([y_a, y_b], axis=-1), w_out)
    return x + rms_norm(y, g_post)

def setup_inputs(seed: int = 0) -> dict:
    key = jax.random.key(seed)
    ks = jax.random.split(key, 7)
    x = jax.random.normal(ks[0], (BATCH, SEQ, D_MODEL), jnp.float32)
    w_in = jax.random.normal(ks[1], (DEPTH, D_MODEL, IN_WIDTH), jnp.float32) * D_MODEL ** -0.5
    b_f = 3.0 + 0.5 * jax.random.normal(ks[2], (DEPTH, FOX_HEADS), jnp.float32)
    sinks = 0.5 * jax.random.normal(ks[3], (DEPTH, SWA_Q_HEADS), jnp.float32)
    w_out = jax.random.normal(ks[4], (DEPTH, MIX_WIDTH, D_MODEL), jnp.float32) * MIX_WIDTH ** -0.5
    g_pre = 1.0 + 0.02 * jax.random.normal(ks[5], (DEPTH, D_MODEL), jnp.float32)
    g_post = 1.0 + 0.02 * jax.random.normal(ks[6], (DEPTH, D_MODEL), jnp.float32)
    return {"x": x, "w_in": w_in, "b_f": b_f, "sinks": sinks, "w_out": w_out,
            "g_pre": g_pre, "g_post": g_post}

def reference(x, w_in, b_f, sinks, w_out, g_pre, g_post):
    positions = jnp.arange(x.shape[1], dtype=jnp.int32)
    h = x
    for layer in range(DEPTH):
        h = hybrid_layer(h, w_in[layer], b_f[layer], sinks[layer], w_out[layer],
                         g_pre[layer], g_post[layer], positions)
    return h


_drawn_inputs = setup_inputs


def setup_inputs(seed=0):
    import zlib

    import numpy as np

    out = dict(_drawn_inputs(seed))
    spreads = {}
    factors = {'sinks': 8.0}
    for name, (base, spread) in spreads.items():
        noise = np.random.default_rng([zlib.crc32(name.encode()), seed]).standard_normal(out[name].shape)
        drawn = base * np.exp(spread * noise) if base else spread * noise
        out[name] = __import__('jax').numpy.asarray(drawn.astype(out[name].dtype))
    for name, factor in factors.items():
        out[name] = (out[name] * factor).astype(out[name].dtype)
    return out
```

```python
from contextlib import ExitStack

import concourse.bass as bass
import numpy as np
from concourse import mybir

P = 128
D_MODEL = 1024
SEQ = 1024
DEPTH = 2
HEAD = 64
CHUNK = 64
SWA_HEADS = 8
FOX_HEADS = 8
SWA_KV = 2
EPS = 1e-6
SCALE = HEAD ** -0.5
KT = D_MODEL // P
NB = SEQ // P
HALF = 512
TILES = 8
SWA_TILES = 4
MASKED = 1e30
FSPLIT = 32

F32 = mybir.dt.float32
F32R = mybir.dt.float32r
BF16 = mybir.dt.bfloat16
ACT = mybir.ActivationFunctionType
ALU = mybir.AluOpType


def chunk_order():
    order = [("K", 0), ("V", 0), ("Q", 0)]
    for t in range(TILES):
        if t >= SWA_TILES:
            order += [("K", t), ("V", t)]
        order.append(("G", t))
        if t + 1 < TILES:
            order.append(("Q", t + 1))
    return order + [("O", c) for c in range(KT)]


CHUNKS = chunk_order()
NCH = len(CHUNKS)
AT = {key: n for n, key in enumerate(CHUNKS)}


class Step:

    def __init__(self, use, index, turns, products):
        self.use = use
        self.index = index
        self.turns = turns
        self.products = products
        self.width = P * len(turns)


class Unit:

    def __init__(self, layer, tile, m, head):
        self.layer, self.tile, self.m, self.head = layer, tile, m, head
        self.index = (layer * TILES + tile) * 8 + 2 * m + head
        self.slot = 2 * m + head
        self.fox = tile >= SWA_TILES
        self.rows = slice(HEAD * head, HEAD * head + HEAD)
        self.score_chunks = [[], []]
        self.steps = []

    def width(self, a):
        qb = 2 * self.m + a
        if self.fox:
            return P * (qb + 1)
        return 2 * P if qb else P

    def key0(self, a):
        return 0 if self.fox else max(2 * self.m + a - 1, 0) * P


class Plan:

    def __init__(self):
        self.units = {}
        self.norm_use, self.v_use, self.out_use = {}, {}, {}
        self.scores_by_tile, self.steps_by_tile, self.first_step_after = {}, {}, {}
        use = score = step = 0
        for layer in range(DEPTH):
            for i in range(NB):
                for g in range(2):
                    self.norm_use[layer, i, g] = use
                    use += 1
            pending = None
            for t in range(TILES):
                fresh = t == 0 or t >= SWA_TILES
                if fresh:
                    if pending is not None:
                        use, step = self.assign_steps(pending, use, step)
                        pending = None
                    for h in range(2):
                        self.v_use[layer, t, h] = use
                        use += 1
                for m in range(4):
                    for head in range(2):
                        u = Unit(layer, t, m, head)
                        self.units[layer, t, u.slot] = u
                        for a in range(2):
                            for c0 in range(0, u.width(a), HALF):
                                u.score_chunks[a].append((score, c0, min(HALF, u.width(a) - c0)))
                                score += 1
                        if pending is not None:
                            use, step = self.assign_steps(pending, use, step)
                        pending = u
                self.scores_by_tile[layer, t] = score
            use, step = self.assign_steps(pending, use, step)
            for c in range(KT):
                for h in range(2):
                    self.out_use[layer, c, h] = use
                    use += 1
        for (layer, t, s), u in self.units.items():
            n = u.steps[-1].index + 1
            self.steps_by_tile[layer, t] = max(self.steps_by_tile.get((layer, t), 0), n)

    def assign_steps(self, u, use, step):
        a0, a1 = 2 * u.m, 2 * u.m + 1
        if u.fox:
            for i in range(u.m + 1):
                k0, k1 = 2 * i, 2 * i + 1
                if i < u.m:
                    turns = [(0, k0 * P), (1, k0 * P), (0, k1 * P), (1, k1 * P)]
                    products = [(k0, 0, 2 * P, 0), (k1, 2 * P, 2 * P, 0)]
                else:
                    turns = [(0, k0 * P), (1, k0 * P), (1, k1 * P)]
                    products = [(k0, 0, 2 * P, 0), (k1, 2 * P, P, P)]
                u.steps.append(Step(use, step, turns, products))
                use, step = use + 1, step + 1
        else:
            turns = [(0, P if u.m else 0), (1, 0), (1, P)]
            products = [(a0, 0, 2 * P, 0), (a1, 2 * P, P, P)]
            if u.m:
                turns.append((0, 0))
                products.append((a0 - 1, 3 * P, P, 0))
            u.steps.append(Step(use, step, turns, products))
            use, step = use + 1, step + 1
        return use, step


def fillers(t):
    return [("G", t), ("Q", t + 1)] if t + 1 < TILES else [("G", t)]


KSTEPS_A_SLOT = 4


def finished_halves(t, slot):
    n = KSTEPS_A_SLOT * (slot + 1) // KT - 1
    if KSTEPS_A_SLOT * (slot + 1) % KT or n >= 2 * len(fillers(t)):
        return []
    return [(fillers(t)[n // 2], n % 2)]


def hybrid_trunk(nc, x, w_chunks, w_gates, b_f, sinks, g_pre, g_post, rotary, ident_in,
                 causal_in, window_in, out):
    plan = Plan()
    with ExitStack() as ctx:
        def sb(name, shape, dt=F32):
            return ctx.enter_context(nc.sbuf_tensor(name, shape, dt))

        def bank(name):
            return ctx.enter_context(nc.psum_tensor(name, [P, HALF], F32))

        def sem(name):
            return ctx.enter_context(nc.semaphore(name))

        trunk = nc.dram_tensor("trunk", [DEPTH, SEQ, D_MODEL], F32).ap()
        c_dram = nc.dram_tensor("c_dram", [DEPTH, FOX_HEADS, SEQ], F32).ap()

        act_hi = sb("act_hi", [P, KT, SEQ], F32R)
        act_lo = sb("act_lo", [P, KT, SEQ], F32R)
        mixed = sb("mixed", [P, KT, SEQ])
        w_raw = sb("w_raw", [P, 2, KT, P])
        w_hi = sb("w_hi", [P, 2, KT, P], F32R)
        w_lo = sb("w_lo", [P, 2, KT, P], F32R)
        f_raw = sb("f_raw", [P, KT, FOX_HEADS])
        f_w = sb("f_w", [P, KT, FSPLIT + FOX_HEADS], F32R)
        q_hi = sb("q_hi", [P, 2, SEQ], F32R)
        q_lo = sb("q_lo", [P, 2, SEQ], F32R)
        k_hi = sb("k_hi", [P, SEQ], F32R)
        k_lo = sb("k_lo", [P, SEQ], F32R)
        v_sb = sb("v_sb", [P, NB, 4 * HEAD], F32R)
        prob = sb("prob", [P, 4, SEQ])
        pt_hi = sb("pt_hi", [P, 2, HALF], F32R)
        pt_lo = sb("pt_lo", [P, 2, HALF], F32R)
        posb = sb("posb", [P, 2, SEQ])
        gains = sb("gains", [P, 2, D_MODEL])
        rope = sb("rope", [P, 2, HALF])
        gate_t = sb("gate_t", [P, HALF])
        o_tmp = sb("o_tmp", [P, 2, 2 * P])
        ident = sb("ident", [P, P])
        ident_bf = sb("ident_bf", [P, P], BF16)
        causal = sb("causal", [P, P], BF16)
        window = sb("window", [P, 2 * P])
        sink_c = sb("sink_c", [P, DEPTH, SWA_HEADS])
        bf_c = sb("bf_c", [FOX_HEADS, DEPTH])
        half_c = sb("half_c", [P, 1])
        peak = sb("peak", [P, 4, 2])
        nmax = sb("nmax", [P, 4])
        rsum = sb("rsum", [P, 4])
        esink = sb("esink", [P, 4])
        rden = sb("rden", [P, 4])
        stat = sb("stat", [P, 2 * DEPTH * NB, 3])

        proj = [bank(f"proj{i}") for i in range(2)]
        score = [bank(f"score{i}") for i in range(2)]
        turn = [bank(f"turn{i}") for i in range(2)]
        mix = [bank(f"mix{i}") for i in range(2)]

        consts_loaded = sem("consts_loaded")
        consts_set = sem("consts_set")
        masks_set = sem("masks_set")
        gains_loaded = [sem(f"gains_loaded{i}") for i in range(2)]
        x_loaded = [sem(f"x_loaded{i}") for i in range(2)]
        posb_loaded = sem("posb_loaded")
        w_loaded = [sem(f"w_loaded{i}") for i in range(2)]
        f_loaded = sem("f_loaded")
        w_hi_done = sem("w_hi_done")
        w_split = sem("w_split")
        f_hi_done = sem("f_hi_done")
        f_split = sem("f_split")
        x_squared = sem("x_squared")
        ms_ready = sem("ms_ready")
        rstd_ready = sem("rstd_ready")
        xn_ready = sem("xn_ready")
        y_scaled = sem("y_scaled")
        x_ready = sem("x_ready")
        x_stored = [sem(f"x_stored{i}") for i in range(2)]
        h_hi = sem("h_hi")
        proj_done = [sem(f"proj_done{i}") for i in range(2)]
        proj_free = [sem(f"proj_free{i}") for i in range(2)]
        proj_hi = sem("proj_hi")
        rope_mul = sem("rope_mul")
        rope_sum = sem("rope_sum")
        v_hi = sem("v_hi")
        gate_act = sem("gate_act")
        z_ready = sem("z_ready")
        e_ready = sem("e_ready")
        c_step = sem("c_step")
        c_stored = sem("c_stored")
        turn_done = sem("turn_done")
        turn_free = sem("turn_free")
        score_done = sem("score_done")
        score_free = sem("score_free")
        nmax_ready = sem("nmax_ready")
        exp_done = sem("exp_done")
        sink_done = sem("sink_done")
        den_ready = sem("den_ready")
        rden_ready = sem("rden_ready")
        prob_ready = sem("prob_ready")
        pt_hi_done = sem("pt_hi_done")
        pv_done = sem("pv_done")
        o_copied = sem("o_copied")
        o_summed = sem("o_summed")
        o_ready = sem("o_ready")
        y_hi_done = sem("y_hi_done")
        y_ready = sem("y_ready")

        N_CONST = 5
        SCAN = [1 << j for j in range(10)]
        N_C = 3 + len(SCAN)
        assert SCAN[-1] * 2 == SEQ
        N_PROJ = NCH + 1
        N_POSB = 16 * (1 + 2 * (TILES - SWA_TILES))

        block = ctx.enter_context(nc.Block())

        def proj_count(g):
            return g + g // NCH + 2

        def number(layer, chunk):
            return layer * NCH + AT[chunk]

        def kq_index(layer, chunk, h):
            kq = [c for c in CHUNKS if c[0] in "KQ"]
            return 2 * (layer * len(kq) + kq.index(chunk)) + h

        def rope_index(layer, chunk, h):
            rotated = [c for c in CHUNKS if c[0] in "KQ" and c[1] < SWA_TILES]
            return 2 * (layer * len(rotated) + rotated.index(chunk)) + h

        def values_of(layer, t):
            return plan.v_use[layer, t if t >= SWA_TILES else 0, 0]

        def split_slots(slot):
            halves = [(t, h) for t in range(TILES - 1) for h in range(2)]
            return halves[4 * (slot - 4):4 * (slot - 3)] if slot >= 4 else []

        last_turn = {u.index: u.steps[-1].use + 1 for u in plan.units.values()}

        def values_count(layer, t, h):
            fresh = 1 + TILES - SWA_TILES
            return 2 * (layer * fresh + (0 if t < SWA_TILES else t - SWA_TILES + 1)) + h + 1

        def sinks_before(u):
            return 2 * ((u.layer * SWA_TILES + u.tile) * 8 + u.slot)

        def head_of(t, head):
            return t + SWA_TILES * head

        @block.sync
        def _(sp):
            sp.dma_start(ident[:], ident_in).then_inc(consts_loaded, 16)
            sp.dma_start(window[:], window_in).then_inc(consts_loaded, 16)
            sp.dma_start(gate_t[:, 0:P], causal_in).then_inc(consts_loaded, 16)
            sp.dma_start(sink_c[:], sinks.rearrange("(o l) h -> o l h", o=1).broadcast_to(
                [P, DEPTH, SWA_HEADS])).then_inc(consts_loaded, 16)
            sp.dma_start(bf_c[:], b_f).then_inc(consts_loaded, 16)
            sp.dma_start(gains[:, 0], g_pre[0:1].broadcast_to([P, D_MODEL])).then_inc(
                gains_loaded[0], 16)

            def weights(layer, n):
                g = layer * NCH + n
                if g >= 2:
                    sp.wait_ge(w_split, g - 1)
                sp.dma_start(w_raw[:, g % 2], w_chunks[layer, n]).then_inc(w_loaded[g % 2], 16)

            def x_rows(layer, i):
                src = x if layer == 0 else trunk[layer - 1]
                sp.dma_start(prob[:, i % 2], src[i * P:(i + 1) * P]).then_inc(x_loaded[i % 2], 16)

            def store(layer, i):
                sp.wait_ge(x_ready, layer * NB + i + 1)
                dst = trunk[layer] if layer + 1 < DEPTH else out
                sp.dma_start(dst[i * P:(i + 1) * P], prob[:, i % 2]).then_inc(x_stored[i % 2], 16)

            for i in range(NB):
                if i >= 2:
                    sp.wait_ge(xn_ready, i - 1)
                x_rows(0, i)
                if i == 0:
                    sp.dma_start(f_raw[:], w_gates[0]).then_inc(f_loaded, 16)
                if i == 1:
                    weights(0, 0)
                    weights(0, 1)
                    sp.dma_start(posb[:], rotary).then_inc(posb_loaded, 16)
            for layer in range(DEPTH):
                if layer:
                    sp.wait_ge(score_free, plan.scores_by_tile[layer - 1, TILES - 1])
                    sp.dma_start(posb[:], rotary).then_inc(posb_loaded, 16)
                for n in range(2, NCH):
                    if n == AT["G", 2]:
                        sp.wait_ge(c_step, (layer + 1) * N_C)
                        sp.dma_start(c_dram[layer], gains[0:FOX_HEADS, 0]).then_inc(c_stored, 16)
                        sp.wait_ge(c_stored, 16 * (layer + 1))
                        sp.dma_start(gains[:, 1], g_post[layer:layer + 1].broadcast_to(
                            [P, D_MODEL])).then_inc(gains_loaded[1], 16)
                        if layer + 1 < DEPTH:
                            sp.wait_ge(f_split, layer + 1)
                            sp.dma_start(f_raw[:], w_gates[layer + 1]).then_inc(f_loaded, 16)
                            sp.dma_start(gains[:, 0], g_pre[layer + 1:layer + 2].broadcast_to(
                                [P, D_MODEL])).then_inc(gains_loaded[0], 16)
                    for t in range(SWA_TILES, TILES):
                        if n == AT["K", t] + 3:
                            sp.wait_ge(score_free, plan.scores_by_tile[layer, t - 1])
                            j = 2 * (t - SWA_TILES)
                            for h in range(2):
                                sp.dma_start(posb[:, h], c_dram[layer, j + h:j + h + 1].broadcast_to(
                                    [P, SEQ])).then_inc(posb_loaded, 16)
                    weights(layer, n)
                if layer + 1 < DEPTH:
                    weights(layer + 1, 0)
                    weights(layer + 1, 1)
                sp.wait_ge(turn_done, plan.out_use[layer, 0, 0])
                for i in range(2):
                    x_rows(layer, i)
                for i in range(NB):
                    store(layer, i)
                    if i + 2 < NB:
                        if layer + 1 < DEPTH:
                            sp.wait_ge(xn_ready, (layer + 1) * NB + i + 1)
                        sp.wait_ge(x_stored[i % 2], 16 * (layer * NB // 2 + i // 2 + 1))
                        x_rows(layer, i + 2)
            for i in range(2):
                sp.wait_ge(x_stored[i], 16 * DEPTH * NB // 2)

        @block.gpsimd
        def _(pool):
            pool.memset(half_c[:], -0.5).then_inc(consts_set, 1)
            pool.memset(f_w[:].bitcast(F32), 0.0).then_inc(consts_set, 1)
            pool.wait_ge(consts_set, 2)

            def gate_weights(layer):
                pool.wait_ge(f_loaded, 16 * (layer + 1))
                if layer:
                    pool.wait_ge(proj_done[1], (layer - 1) * N_PROJ + 1)
                pool.tensor_copy(f_w[:, :, 0:FOX_HEADS], f_raw[:]).then_inc(f_hi_done, 1)
                pool.wait_ge(f_hi_done, layer + 1)
                pool.tensor_tensor(f_w[:, :, FSPLIT:FSPLIT + FOX_HEADS], f_raw[:],
                                   f_w[:, :, 0:FOX_HEADS].bitcast(F32), ALU.subtract).then_inc(f_split, 1)

            def split(g):
                s = g % 2
                pool.wait_ge(w_loaded[s], 16 * (g // 2 + 1))
                if g >= 2:
                    pool.wait_ge(proj_done[1], proj_count(g - 2))
                pool.tensor_copy(w_hi[:, s], w_raw[:, s]).then_inc(w_hi_done, 1)
                pool.wait_ge(w_hi_done, g + 1)
                pool.tensor_tensor(w_lo[:, s], w_raw[:, s], w_hi[:, s].bitcast(F32),
                                   ALU.subtract).then_inc(w_split, 1)

            def rstd(n):
                pool.wait_ge(ms_ready, n + 1)
                pool.tensor_tensor(stat[:, n, 2:3], stat[:, n, 1:2], half_c[:],
                                   ALU.pow).then_inc(rstd_ready, 1)

            gate_weights(0)
            for i in range(NB):
                rstd(i)
                if i in (1, 3):
                    split(i // 2)
            n = NB
            for layer in range(DEPTH):
                for c in range(2, NCH):
                    split(layer * NCH + c)
                if layer + 1 < DEPTH:
                    gate_weights(layer + 1)
                    split((layer + 1) * NCH)
                    split((layer + 1) * NCH + 1)
                for i in range(NB):
                    rstd(n)
                    n += 1
                    if layer + 1 < DEPTH:
                        rstd(n)
                        n += 1

        @block.tensor
        def _(pe):
            pe.wait_ge(consts_loaded, 16 * N_CONST)
            pe.wait_ge(masks_set, 2)

            def take_turn_bank(use):
                if use >= 2:
                    pe.wait_ge(turn_free, use - 1)
                return turn[use % 2]

            def norm_turns(layer, i):
                pe.wait_ge(xn_ready, layer * NB + i + 1)
                for g in range(2):
                    b = take_turn_bank(plan.norm_use[layer, i, g])
                    for j in range(4):
                        k = 4 * g + j
                        mm = nc.tensor.transpose(b[:, j * P:(j + 1) * P],
                                                 prob[:, 2 + i % 2, k * P:(k + 1) * P], ident[:])
                    mm.then_inc(turn_done, 1)

            def forget_logits(layer):
                pe.wait_ge(f_split, layer + 1)
                for h in range(2):
                    pe.wait_ge(turn_free, plan.norm_use[layer, 4 * h + 3, 1] + 1)
                    if layer:
                        pe.wait_ge(proj_free[h], layer * N_PROJ)
                    cols = slice(h * HALF, (h + 1) * HALF)
                    for k in range(KT):
                        nc.tensor.matmul(proj[h][0:FSPLIT + FOX_HEADS, :], f_w[:, k, :],
                                         act_hi[:, k, cols], start=(k == 0), stop=False,
                                         skip_group_check=True)
                    for k in range(KT):
                        mm = nc.tensor.matmul(proj[h][0:FOX_HEADS, :], f_w[:, k, 0:FOX_HEADS],
                                              act_lo[:, k, cols], start=False, stop=(k == KT - 1),
                                              skip_group_check=True)
                    mm.then_inc(proj_done[h], 1)

            def project(layer, chunk, h, k0, k1):
                g = number(layer, chunk)
                s = g % 2
                cols = slice(h * HALF, (h + 1) * HALF)
                if k0 == 0:
                    if h == 0:
                        pe.wait_ge(w_split, g + 1)
                    pe.wait_ge(proj_free[h], proj_count(g) - 1)
                for k in range(k0, k1):
                    if chunk[0] == "O":
                        pe.wait_ge(y_ready, 2 * (layer * TILES + k) + h + 1)
                    nc.tensor.matmul(proj[h][:], w_hi[:, s, k], act_hi[:, k, cols],
                                     start=(k == 0), stop=False)
                    nc.tensor.matmul(proj[h][:], w_hi[:, s, k], act_lo[:, k, cols],
                                     start=False, stop=False)
                    mm = nc.tensor.matmul(proj[h][:], w_lo[:, s, k], act_hi[:, k, cols],
                                          start=False, stop=(k == KT - 1))
                if k1 == KT:
                    mm.then_inc(proj_done[h], 1)

            def whole(layer, chunk):
                for h in range(2):
                    project(layer, chunk, h, 0, KT)

            def fill(layer, t, i0, i1):
                for i in range(i0, i1):
                    if i < 2 * KT * len(fillers(t)):
                        c, r = divmod(i, 2 * KT)
                        project(layer, fillers(t)[c], r // KT, r % KT, r % KT + 1)

            def staged_turns(layer, kind, t, uses):
                for h in range(2):
                    pe.wait_ge(proj_free[h], proj_count(number(layer, (kind, t))))
                    b = take_turn_bank(uses[layer, t, h])
                    for j in range(4):
                        mm = nc.tensor.transpose(b[:, j * P:(j + 1) * P],
                                                 rope[:, h, j * P:(j + 1) * P], ident[:])
                    mm.then_inc(turn_done, 1)

            def scores(u):
                q = u.tile % 2
                if u.slot == 0:
                    for h in range(2):
                        pe.wait_ge(proj_free[h], proj_count(number(u.layer, ("Q", u.tile))))
                        if u.fox:
                            pe.wait_ge(proj_free[h], proj_count(number(u.layer, ("K", u.tile))))
                for a in range(2):
                    qb = 2 * u.m + a
                    qc = slice(qb * P, (qb + 1) * P)
                    for index, c0, n in u.score_chunks[a]:
                        if index >= 2:
                            pe.wait_ge(score_free, index - 1)
                        b = score[index % 2]
                        kc = slice(u.key0(a) + c0, u.key0(a) + c0 + n)
                        diagonal = u.fox and c0 + n == u.width(a)
                        nc.tensor.matmul(b[:, 0:n], q_hi[u.rows, q, qc], k_hi[u.rows, kc],
                                         start=True, stop=False, skip_group_check=True)
                        nc.tensor.matmul(b[:, 0:n], q_hi[u.rows, q, qc], k_lo[u.rows, kc],
                                         start=False, stop=False, skip_group_check=True)
                        mm = nc.tensor.matmul(b[:, 0:n], q_lo[u.rows, q, qc], k_hi[u.rows, kc],
                                              start=False, stop=not diagonal, skip_group_check=True)
                        if diagonal:
                            mm = nc.tensor.matmul(b[:, n - P:n], ident_bf[:], causal[:],
                                                  start=False, stop=True, skip_group_check=True)
                        mm.then_inc(score_done, 1)

            def turn_probs(u, step):
                b = take_turn_bank(step.use)
                for j, (a, col) in enumerate(step.turns):
                    mm = nc.tensor.transpose(b[:, j * P:(j + 1) * P],
                                             prob[:, 2 * (u.index % 2) + a, col:col + P], ident[:])
                mm.then_inc(turn_done, 1)

            def multiply_values(u, step):
                o = mix[u.index % 2]
                first, last = step is u.steps[0], step is u.steps[-1]
                if first and u.index >= 2:
                    pe.wait_ge(o_ready, u.index - 1)
                if first and u.slot == 0:
                    pe.wait_ge(turn_free, values_of(u.layer, u.tile) + 2)
                pe.wait_ge(turn_free, step.use + 1)
                s = step.index % 2
                vc = slice(2 * HEAD * u.head, 2 * HEAD * (u.head + 1))
                for j, (kb, col, n, oc) in enumerate(step.products):
                    nc.tensor.matmul(o[:, oc:oc + n], v_sb[:, kb, vc], pt_hi[:, s, col:col + n],
                                     start=(first and j == 0), stop=False, skip_group_check=True)
                    mm = nc.tensor.matmul(o[:, oc:oc + n], v_sb[:, kb, vc], pt_lo[:, s, col:col + n],
                                          start=False, stop=(last and j == len(step.products) - 1),
                                          skip_group_check=True)
                mm.then_inc(pv_done, 1)

            def finish_unit(u, between=None):
                pe.wait_ge(prob_ready, 2 * u.index + 2)
                for i, step in enumerate(u.steps):
                    turn_probs(u, step)
                    if i == 0 and between is not None:
                        between()
                    if i:
                        multiply_values(u, u.steps[i - 1])
                return u.steps[-1]

            for layer in range(DEPTH):
                for i in range(NB):
                    norm_turns(layer, i)
                forget_logits(layer)
                whole(layer, ("K", 0))
                whole(layer, ("V", 0))
                project(layer, ("Q", 0), 0, 0, KT)
                staged_turns(layer, "V", 0, plan.v_use)
                project(layer, ("Q", 0), 1, 0, KT)
                before = None
                for t in range(TILES):
                    if t >= SWA_TILES:
                        project(layer, ("K", t), 0, 0, KT)
                        last = finish_unit(before)
                        project(layer, ("K", t), 1, 0, KT)
                        multiply_values(before, last)
                        before = None
                        whole(layer, ("V", t))
                        staged_turns(layer, "V", t, plan.v_use)
                    for slot in range(8):
                        u = plan.units[layer, t, slot]
                        f0 = KSTEPS_A_SLOT * slot
                        scores(u)
                        fill(layer, t, f0, f0 + 1)
                        if before is not None:
                            last = finish_unit(before, lambda: fill(layer, t, f0 + 1, f0 + 2))
                            fill(layer, t, f0 + 2, f0 + 4)
                            multiply_values(before, last)
                        else:
                            fill(layer, t, f0 + 1, f0 + 4)
                        before = u
                last = finish_unit(before)
                multiply_values(before, last)
                for c in range(KT):
                    whole(layer, ("O", c))
                    staged_turns(layer, "O", c, plan.out_use)

        @block.scalar
        def _(act):
            act.wait_ge(consts_loaded, 16 * N_CONST)

            def norm_squares(layer, i, n):
                if layer == 0:
                    act.wait_ge(x_loaded[i % 2], 16 * (i // 2 + 1))
                else:
                    act.wait_ge(x_ready, (layer - 1) * NB + i + 1)
                if i >= 2:
                    act.wait_ge(turn_done, plan.norm_use[layer, i - 2, 1] + 1)
                nc.scalar.activation(prob[:, 2 + i % 2], prob[:, i % 2], ACT.Square,
                                     accum_out=stat[:, n, 0:1]).then_inc(x_squared, 1)

            def norm_hi(layer, i):
                for g in range(2):
                    use = plan.norm_use[layer, i, g]
                    act.wait_ge(turn_done, use + 1)
                    nc.scalar.activation(act_hi[:, 4 * g:4 * g + 4, i * P:(i + 1) * P],
                                         turn[use % 2][:].rearrange("p (k s) -> p k s", k=4),
                                         ACT.Copy).then_inc(h_hi, 1)

            def forget_exps(layer):
                act.wait_ge(z_ready, 2 * (layer + 1))
                row = gains[0:FOX_HEADS, 1]
                nc.scalar.activation(row, row, ACT.Exp).then_inc(e_ready, 1)
                act.wait_ge(e_ready, 2 * layer + 1)
                nc.scalar.activation(row, row, ACT.Ln, bias=1.0).then_inc(e_ready, 1)

            def round_half(layer, chunk, h):
                kind, t = chunk
                cols = slice(h * HALF, (h + 1) * HALF)
                dst = k_hi[:, cols] if kind == "K" else q_hi[:, t % 2, cols]
                old = t - 1 if kind == "K" else t - 2
                if old >= 0:
                    act.wait_ge(score_done, plan.scores_by_tile[layer, old])
                elif layer:
                    act.wait_ge(score_done, plan.scores_by_tile[layer - 1, TILES - 1])
                if t < SWA_TILES:
                    act.wait_ge(rope_sum, rope_index(layer, chunk, h) + 1)
                    src = rope[:, 0]
                else:
                    act.wait_ge(proj_done[h], proj_count(number(layer, chunk)))
                    src = proj[h][:]
                nc.scalar.activation(dst, src, ACT.Copy,
                                     scale=SCALE if kind == "Q" else 1.0).then_inc(proj_hi, 1)

            def gate_half(layer, t, h):
                act.wait_ge(proj_done[h], proj_count(number(layer, ("G", t))))
                if h or layer or t:
                    last = number(layer, ("G", t)) if h else (
                        number(layer, ("G", t - 1)) if t else number(layer - 1, ("G", TILES - 1)))
                    act.wait_ge(proj_free[1 - h], proj_count(last))
                nc.scalar.activation(gate_t[:], proj[h][:], ACT.Tanh, scale=0.5).then_inc(gate_act, 1)

            def fillers_done(layer, t, slot):
                for chunk, h in finished_halves(t, slot):
                    if chunk[0] == "G":
                        gate_half(layer, chunk[1], h)
                    else:
                        round_half(layer, chunk, h)

            def value_hi(layer, t):
                for h in range(2):
                    use = plan.v_use[layer, t, h]
                    act.wait_ge(turn_done, use + 1)
                    if h == 0 and (layer or t):
                        prev = (layer, t - 1) if t else (layer - 1, TILES - 1)
                        act.wait_ge(pv_done, plan.steps_by_tile[prev])
                    b = turn[use % 2][:].rearrange("p (s d) -> p s d", s=4)
                    kbs = slice(4 * h, 4 * h + 4)
                    nc.scalar.activation(v_sb[:, kbs, 0:HEAD], b[:, :, 0:HEAD], ACT.Copy)
                    nc.scalar.activation(v_sb[:, kbs, 3 * HEAD:4 * HEAD], b[:, :, HEAD:P],
                                         ACT.Copy).then_inc(v_hi, 1)

            def exponentials(u):
                for a in range(2):
                    n = 2 * u.index + a
                    s = n % 4
                    act.wait_ge(nmax_ready, n + 1)
                    row = prob[:, s, 0:u.width(a)]
                    nc.scalar.activation(row, row, ACT.Exp, bias=nmax[:, s:s + 1],
                                         accum_out=rsum[:, s:s + 1]).then_inc(exp_done, 1)
                    if not u.fox:
                        h = head_of(u.tile, u.head)
                        nc.scalar.activation(esink[:, s:s + 1], sink_c[:, u.layer, h:h + 1],
                                             ACT.Exp, bias=nmax[:, s:s + 1]).then_inc(sink_done, 1)

            def probs_hi(u):
                for step in u.steps:
                    act.wait_ge(turn_done, step.use + 1)
                    if step.index >= 2:
                        act.wait_ge(pv_done, step.index - 1)
                    nc.scalar.activation(pt_hi[:, step.index % 2, 0:step.width],
                                         turn[step.use % 2][:, 0:step.width],
                                         ACT.Copy).then_inc(pt_hi_done, 1)

            def copy_output(u):
                act.wait_ge(pv_done, u.steps[-1].index + 1)
                if u.index >= 2:
                    act.wait_ge(o_ready, u.index - 1)
                other = slice(HEAD, P) if u.head == 0 else slice(0, HEAD)
                nc.scalar.activation(o_tmp[u.rows, 0], mix[u.index % 2][other, 0:2 * P],
                                     ACT.Copy).then_inc(o_copied, 1)

            def mixed_hi(layer, t, h):
                act.wait_ge(o_ready, (layer * TILES + t) * 8 + 4 * (h + 1))
                act.wait_ge(proj_done[1], proj_count(number(layer, ("G", TILES - 1))))
                cols = slice(h * HALF, (h + 1) * HALF)
                nc.scalar.activation(act_hi[:, t, cols], mixed[:, t, cols],
                                     ACT.Copy).then_inc(y_hi_done, 1)

            def out_squares(layer, i, n):
                act.wait_ge(turn_free, plan.out_use[layer, KT - 1, 1] + 1)
                if i >= 2 and layer + 1 < DEPTH:
                    act.wait_ge(turn_done, plan.norm_use[layer + 1, i - 2, 1] + 1)
                elif i >= 2:
                    act.wait_ge(x_squared, n)
                nc.scalar.activation(prob[:, 2 + i % 2], mixed[:, i], ACT.Square,
                                     accum_out=stat[:, n, 0:1]).then_inc(x_squared, 1)

            n = 0
            for i in range(NB):
                norm_squares(0, i, n)
                n += 1
                if i:
                    norm_hi(0, i - 1)
            norm_hi(0, NB - 1)
            for layer in range(DEPTH):
                forget_exps(layer)
                for chunk in (("K", 0), ("Q", 0)):
                    for h in range(2):
                        round_half(layer, chunk, h)
                        if chunk[0] == "Q" and h == 0:
                            value_hi(layer, 0)
                before = None
                for t in range(TILES):
                    if t >= SWA_TILES:
                        round_half(layer, ("K", t), 0)
                        probs_hi(before)
                        round_half(layer, ("K", t), 1)
                        copy_output(before)
                        before = None
                        value_hi(layer, t)
                    for slot in range(8):
                        u = plan.units[layer, t, slot]
                        exponentials(u)
                        if before is not None:
                            probs_hi(before)
                        fillers_done(layer, t, slot)
                        if before is not None:
                            copy_output(before)
                        if t == TILES - 1:
                            for ts, h in split_slots(slot):
                                mixed_hi(layer, ts, h)
                        before = u
                probs_hi(before)
                copy_output(before)
                for h in range(2):
                    mixed_hi(layer, TILES - 1, h)
                for i in range(NB):
                    out_squares(layer, i, n)
                    n += 1
                    if layer + 1 < DEPTH:
                        norm_squares(layer + 1, i, n)
                        n += 1
                        norm_hi(layer + 1, i)

        @block.vector
        def _(dve):
            dve.wait_ge(consts_loaded, 16 * N_CONST)
            nc.vector.tensor_copy(ident_bf[:], ident[:]).then_inc(masks_set, 1)
            nc.vector.tensor_copy(causal[:], gate_t[:, 0:P]).then_inc(masks_set, 1)

            def mean_square(n):
                dve.wait_ge(x_squared, n + 1)
                nc.vector.tensor_scalar(stat[:, n, 1:2], stat[:, n, 0:1], 1.0 / D_MODEL, EPS,
                                        ALU.mult, ALU.add).then_inc(ms_ready, 1)
                dve.wait_ge(rstd_ready, n + 1)

            def norm_rows(layer, i, n):
                mean_square(n)
                if i == 0:
                    dve.wait_ge(gains_loaded[0], 16 * (layer + 1))
                nc.vector.scalar_tensor_tensor(prob[:, 2 + i % 2], prob[:, i % 2], stat[:, n, 2:3],
                                               gains[:, 0], ALU.mult, ALU.mult).then_inc(xn_ready, 1)

            def norm_lo(layer, i):
                for g in range(2):
                    use = plan.norm_use[layer, i, g]
                    ks = slice(4 * g, 4 * g + 4)
                    rows = slice(i * P, (i + 1) * P)
                    dve.wait_ge(h_hi, 2 * (layer * NB + i) + g + 1)
                    nc.vector.tensor_tensor(act_lo[:, ks, rows],
                                            turn[use % 2][:].rearrange("p (k s) -> p k s", k=4),
                                            act_hi[:, ks, rows].bitcast(F32),
                                            ALU.subtract).then_inc(turn_free, 1)

            def forget_logits(layer):
                for h in range(2):
                    cols = slice(h * HALF, (h + 1) * HALF)
                    z, minus = gains[0:FOX_HEADS, 0, cols], gains[0:FOX_HEADS, 1, cols]
                    dve.wait_ge(proj_done[h], layer * N_PROJ + 1)
                    nc.vector.tensor_scalar(z, proj[h][FSPLIT:FSPLIT + FOX_HEADS, :],
                                            bf_c[:, layer:layer + 1], None,
                                            ALU.add).then_inc(c_step, 1)
                    dve.wait_ge(c_step, layer * N_C + h + 1)
                    nc.vector.tensor_tensor(z, proj[h][0:FOX_HEADS, :], z,
                                            ALU.add).then_inc(proj_free[h], 1)
                    dve.wait_ge(proj_free[h], layer * N_PROJ + 1)
                    nc.vector.scalar_tensor_tensor(minus, z, -1.0, z, ALU.mult,
                                                   ALU.min).then_inc(z_ready, 1)

            def forget_logs(layer):
                dve.wait_ge(e_ready, 2 * (layer + 1))
                nc.vector.scalar_tensor_tensor(gains[0:FOX_HEADS, 0], gains[0:FOX_HEADS, 0], 0.0,
                                               gains[0:FOX_HEADS, 1], ALU.min,
                                               ALU.subtract).then_inc(c_step, 1)

            def forget_sums(layer, j):
                d = SCAN[j]
                src, dst = gains[0:FOX_HEADS, j % 2], gains[0:FOX_HEADS, 1 - j % 2]
                dve.wait_ge(c_step, layer * N_C + 3 + j)
                nc.vector.tensor_copy(dst[:, 0:d], src[:, 0:d])
                nc.vector.tensor_tensor(dst[:, d:SEQ], src[:, d:SEQ], src[:, 0:SEQ - d],
                                        ALU.add).then_inc(c_step, 1)

            def rotate(layer, chunk, h):
                n = rope_index(layer, chunk, h)
                cols = slice(h * HALF, (h + 1) * HALF)
                dve.wait_ge(proj_done[h], proj_count(number(layer, chunk)))
                dve.wait_ge(posb_loaded, layer * N_POSB + 16)
                if chunk == ("K", 0) and h == 0 and layer:
                    dve.wait_ge(turn_done, plan.out_use[layer - 1, KT - 1, 1] + 1)
                if chunk == ("Q", 0):
                    dve.wait_ge(turn_done, plan.v_use[layer, 0, 1] + 1)
                if h or chunk != ("K", 0):
                    last = chunk if h else ("Q", chunk[1] - 1) if chunk[1] else ("K", 0)
                    dve.wait_ge(proj_free[1 - h], proj_count(number(layer, last)))
                nc.vector.tensor_tensor(rope[:, 0], proj[h][:], posb[:, 0, cols],
                                        ALU.mult).then_inc(rope_mul, 1)
                for q in range(4):
                    to = slice(32 * q, 32 * q + 32)
                    of = slice(32 * (q ^ 1), 32 * (q ^ 1) + 32)
                    nc.vector.tensor_tensor(rope[to, 1], proj[h][of, :], posb[to, 1, cols],
                                            ALU.mult).then_inc(rope_mul, 1)
                dve.wait_ge(rope_mul, 5 * (n + 1))
                nc.vector.tensor_tensor(rope[:, 0], rope[:, 0], rope[:, 1],
                                        ALU.add).then_inc(rope_sum, 1)

            def split_half(layer, chunk, h):
                kind, t = chunk
                cols = slice(h * HALF, (h + 1) * HALF)
                lo = k_lo[:, cols] if kind == "K" else q_lo[:, t % 2, cols]
                hi = k_hi[:, cols] if kind == "K" else q_hi[:, t % 2, cols]
                if t < SWA_TILES:
                    rotate(layer, chunk, h)
                    src = rope[:, 0]
                else:
                    src = proj[h][:]
                dve.wait_ge(proj_hi, kq_index(layer, chunk, h) + 1)
                nc.vector.scalar_tensor_tensor(lo, src, SCALE if kind == "Q" else 1.0,
                                               hi.bitcast(F32), ALU.mult,
                                               ALU.subtract).then_inc(proj_free[h], 1)

            def gate_half(layer, t, h):
                cols = slice(h * HALF, (h + 1) * HALF)
                dve.wait_ge(gate_act, 2 * (layer * TILES + t) + h + 1)
                nc.vector.scalar_tensor_tensor(mixed[:, t, cols], gate_t[:], 1.0, proj[h][:],
                                               ALU.add, ALU.mult).then_inc(proj_free[h], 1)

            def stage_half(layer, kind, t, h):
                dve.wait_ge(proj_done[h], proj_count(number(layer, (kind, t))))
                if kind == "O":
                    dve.wait_ge(turn_done, plan.out_use[layer, t, h] - 1)
                else:
                    if t:
                        dve.wait_ge(turn_done, plan.v_use[layer, t, h] - 1)
                    last = ("Q", SWA_TILES - 1) if t else ("K", 0)
                    dve.wait_ge(proj_free[1], proj_count(number(layer, last)))
                nc.vector.tensor_copy(rope[:, h], proj[h][:]).then_inc(proj_free[h], 1)

            def fillers_done(layer, t, slot):
                for chunk, h in finished_halves(t, slot):
                    if chunk[0] == "G":
                        gate_half(layer, chunk[1], h)
                    else:
                        split_half(layer, chunk, h)

            def value_lo(layer, t):
                for h in range(2):
                    use = plan.v_use[layer, t, h]
                    b = turn[use % 2][:].rearrange("p (s d) -> p s d", s=4)
                    kbs = slice(4 * h, 4 * h + 4)
                    dve.wait_ge(v_hi, values_count(layer, t, h))
                    nc.vector.tensor_tensor(v_sb[:, kbs, HEAD:2 * HEAD], b[:, :, 0:HEAD],
                                            v_sb[:, kbs, 0:HEAD].bitcast(F32), ALU.subtract)
                    nc.vector.tensor_tensor(v_sb[:, kbs, 2 * HEAD:3 * HEAD], b[:, :, HEAD:P],
                                            v_sb[:, kbs, 3 * HEAD:4 * HEAD].bitcast(F32),
                                            ALU.subtract).then_inc(turn_free, 1)

            def bias_scores(u):
                if u.slot == 0:
                    if u.fox:
                        dve.wait_ge(posb_loaded,
                                    u.layer * N_POSB + 16 + 32 * (u.tile - SWA_TILES + 1))
                    elif u.tile == 0 and u.layer:
                        for i in range(2):
                            dve.wait_ge(x_stored[i], 16 * (NB // 2) * u.layer)
                if u.index >= 2:
                    dve.wait_ge(turn_done, last_turn[u.index - 2])
                for a in range(2):
                    s = (2 * u.index + a) % 4
                    for j, (index, c0, n) in enumerate(u.score_chunks[a]):
                        dve.wait_ge(score_done, index + 1)
                        w0 = 2 * P - u.width(a)
                        bias = posb[:, u.head, c0:c0 + n] if u.fox else window[:, w0:w0 + n]
                        nc.vector.tensor_tensor_reduce(prob[:, s, c0:c0 + n], score[index % 2][:, 0:n],
                                                       bias, 1.0, -3e38, ALU.subtract, ALU.max,
                                                       peak[:, s, j:j + 1]).then_inc(score_free, 1)
                for a in range(2):
                    s = (2 * u.index + a) % 4
                    dve.wait_ge(score_free, u.score_chunks[a][-1][0] + 1)
                    if not u.fox:
                        h = head_of(u.tile, u.head)
                        args = (sink_c[:, u.layer, h:h + 1], -1.0, ALU.max, ALU.mult)
                    elif len(u.score_chunks[a]) > 1:
                        args = (peak[:, s, 1:2], -1.0, ALU.max, ALU.mult)
                    else:
                        args = (-1.0, None, ALU.mult)
                    nc.vector.tensor_scalar(nmax[:, s:s + 1], peak[:, s, 0:1],
                                            *args).then_inc(nmax_ready, 1)

            def probs_lo(u):
                for step in u.steps:
                    dve.wait_ge(pt_hi_done, step.index + 1)
                    s = step.index % 2
                    nc.vector.tensor_tensor(pt_lo[:, s, 0:step.width],
                                            turn[step.use % 2][:, 0:step.width],
                                            pt_hi[:, s, 0:step.width].bitcast(F32),
                                            ALU.subtract).then_inc(turn_free, 1)

            def normalise(u):
                for a in range(2):
                    n = 2 * u.index + a
                    s = n % 4
                    dve.wait_ge(exp_done, n + 1)
                    if not u.fox:
                        count = sinks_before(u) + a + 1
                        dve.wait_ge(sink_done, count)
                        nc.vector.tensor_tensor(rsum[:, s:s + 1], rsum[:, s:s + 1],
                                                esink[:, s:s + 1], ALU.add).then_inc(den_ready, 1)
                        dve.wait_ge(den_ready, count)
                    nc.vector.reciprocal(rden[:, s:s + 1], rsum[:, s:s + 1]).then_inc(rden_ready, 1)
                for a in range(2):
                    n = 2 * u.index + a
                    s = n % 4
                    dve.wait_ge(rden_ready, n + 1)
                    row = prob[:, s, 0:u.width(a)]
                    nc.vector.tensor_scalar(row, row, rden[:, s:s + 1], None,
                                            ALU.mult).then_inc(prob_ready, 1)

            def gate_output(u):
                dve.wait_ge(o_copied, u.index + 1)
                nc.vector.tensor_tensor(o_tmp[u.rows, 1], mix[u.index % 2][u.rows, 0:2 * P],
                                        o_tmp[u.rows, 0], ALU.add).then_inc(o_summed, 1)
                dve.wait_ge(o_summed, u.index + 1)
                h = u.m // 2
                dve.wait_ge(proj_free[h], proj_count(number(u.layer, ("G", u.tile))))
                dst = mixed[u.rows, u.tile, 2 * P * u.m:2 * P * (u.m + 1)]
                nc.vector.scalar_tensor_tensor(dst, o_tmp[u.rows, 1], 0.5, dst, ALU.mult,
                                               ALU.mult).then_inc(o_ready, 1)

            def mixed_lo(layer, t, h):
                cols = slice(h * HALF, (h + 1) * HALF)
                dve.wait_ge(y_hi_done, 2 * (layer * TILES + t) + h + 1)
                nc.vector.tensor_tensor(act_lo[:, t, cols], mixed[:, t, cols],
                                        act_hi[:, t, cols].bitcast(F32),
                                        ALU.subtract).then_inc(y_ready, 1)

            def out_rows(layer, c):
                for h in range(2):
                    use = plan.out_use[layer, c, h]
                    dve.wait_ge(turn_done, use + 1)
                    nc.vector.tensor_copy(mixed[:, 4 * h:4 * h + 4, c * P:(c + 1) * P],
                                          turn[use % 2][:].rearrange("p (s d) -> p s d", s=4)
                                          ).then_inc(turn_free, 1)

            def add_rows(layer, i, n):
                mean_square(n)
                if i == 0:
                    dve.wait_ge(gains_loaded[1], 16 * (layer + 1))
                dve.wait_ge(x_loaded[i % 2], 16 * (NB // 2 * (layer + 1) + i // 2 + 1))
                nc.vector.scalar_tensor_tensor(mixed[:, i], mixed[:, i], stat[:, n, 2:3], gains[:, 1],
                                               ALU.mult, ALU.mult).then_inc(y_scaled, 1)
                dve.wait_ge(y_scaled, layer * NB + i + 1)
                nc.vector.tensor_tensor(prob[:, i % 2], prob[:, i % 2], mixed[:, i],
                                        ALU.add).then_inc(x_ready, 1)

            n = 0
            for i in range(NB):
                norm_rows(0, i, n)
                n += 1
                if i:
                    norm_lo(0, i - 1)
            norm_lo(0, NB - 1)
            for layer in range(DEPTH):
                forget_logits(layer)
                forget_logs(layer)
                for h in range(2):
                    split_half(layer, ("K", 0), h)
                for h in range(2):
                    stage_half(layer, "V", 0, h)
                split_half(layer, ("Q", 0), 0)
                value_lo(layer, 0)
                split_half(layer, ("Q", 0), 1)
                before = None
                for t in range(TILES):
                    if t >= SWA_TILES:
                        split_half(layer, ("K", t), 0)
                        probs_lo(before)
                        split_half(layer, ("K", t), 1)
                        gate_output(before)
                        before = None
                        for h in range(2):
                            stage_half(layer, "V", t, h)
                        value_lo(layer, t)
                    for slot in range(8):
                        u = plan.units[layer, t, slot]
                        bias_scores(u)
                        if before is not None:
                            probs_lo(before)
                        fillers_done(layer, t, slot)
                        normalise(u)
                        if before is not None:
                            gate_output(before)
                        if 8 * t + slot < len(SCAN):
                            forget_sums(layer, 8 * t + slot)
                        if t == TILES - 1:
                            for ts, h in split_slots(slot):
                                mixed_lo(layer, ts, h)
                        before = u
                probs_lo(before)
                gate_output(before)
                for h in range(2):
                    mixed_lo(layer, TILES - 1, h)
                for c in range(KT):
                    for h in range(2):
                        stage_half(layer, "O", c, h)
                    out_rows(layer, c)
                for i in range(NB):
                    add_rows(layer, i, n)
                    n += 1
                    if layer + 1 < DEPTH:
                        norm_rows(layer + 1, i, n)
                        n += 1
                        norm_lo(layer + 1, i)


def w_in_columns():
    swa, kv, fox = SWA_HEADS * HEAD, SWA_KV * HEAD, FOX_HEADS * HEAD
    starts = np.cumsum([0, swa, kv, kv, swa, fox, fox, fox, FOX_HEADS])
    qa, ka, va, ga, qb, kb, vb, fb, gb = (int(s) for s in starts)

    def pair(base, a, b):
        return [base + HEAD * n + d for n in (a, b) for d in range(HEAD)]

    cols = []
    for kind, t in CHUNKS:
        if kind == "O":
            continue
        if t < SWA_TILES:
            base, heads = {"Q": (qa, (t, t + SWA_TILES)), "G": (ga, (t, t + SWA_TILES)),
                           "K": (ka, (0, 1)), "V": (va, (0, 1))}[kind]
        else:
            j = 2 * (t - SWA_TILES)
            base, heads = {"Q": qb, "K": kb, "V": vb, "G": gb}[kind], (j, j + 1)
        cols.append(pair(base, *heads))
    return cols, fb


def lay_out(w_in, w_out):
    cols, fb = w_in_columns()
    w = w_in.reshape(DEPTH, KT, P, -1)
    chunks = [w[..., c].transpose(0, 2, 1, 3) for c in cols]
    swa_rows = [HEAD * n + d for t in range(SWA_TILES) for n in (t, t + SWA_TILES) for d in range(HEAD)]
    rows = swa_rows + list(range(SWA_HEADS * HEAD, D_MODEL))
    wo = w_out[:, rows].reshape(DEPTH, KT, P, KT, P)
    chunks += [wo[:, :, :, c].transpose(0, 2, 1, 3) for c in range(KT)]
    gates = w[..., fb:fb + FOX_HEADS].transpose(0, 2, 1, 3)
    return np.ascontiguousarray(np.stack(chunks, axis=1)), np.ascontiguousarray(gates)


def constants():
    half = HEAD // 2
    freq = np.float32(10000.0) ** (-np.arange(half, dtype=np.float32) / np.float32(half))
    ang = np.arange(SEQ, dtype=np.float32)[:, None] * freq[None, :]
    cos, sin = np.cos(ang).T, np.sin(ang).T
    rotary = np.stack([np.concatenate([cos] * 4), np.concatenate([-sin, sin] * 2)], axis=1)
    q, k = np.arange(P)[:, None], np.arange(2 * P)[None, :]
    qc, kc = q // CHUNK, k // CHUNK - 2
    return {
        "rotary": rotary.astype(np.float32),
        "ident": np.eye(P, dtype=np.float32),
        "causal": np.where(k[:, :P] <= q, 0.0, -MASKED).astype(np.float32),
        "window": np.where((kc <= qc) & (kc > qc - 2), 0.0, MASKED).astype(np.float32),
    }


def kernel(x, w_in, b_f, sinks, w_out, g_pre, g_post):
    import concourse.bacc as bacc
    from concourse.bass_utils import run_bass_kernel_spmd

    nc = bacc.Bacc("TRN2", target_bir_lowering=False, num_devices=1)
    w_chunks, w_gates = lay_out(np.asarray(w_in), np.asarray(w_out))
    c = constants()
    arrays = {"x_in": np.ascontiguousarray(np.asarray(x)[0]), "w_chunks": w_chunks, "w_gates": w_gates,
              "b_f_in": np.ascontiguousarray(np.asarray(b_f).T), "sinks_in": np.ascontiguousarray(sinks),
              "g_pre_in": np.ascontiguousarray(g_pre), "g_post_in": np.ascontiguousarray(g_post),
              "rotary_in": c["rotary"], "ident_in": c["ident"],
              "causal_in": c["causal"], "window_in": c["window"]}
    args = [nc.dram_tensor(name, a.shape, mybir.dt.from_np(a.dtype), kind="ExternalInput").ap()
            for name, a in arrays.items()]
    out = nc.dram_tensor("rows_out", (SEQ, D_MODEL), F32, kind="ExternalOutput").ap()
    hybrid_trunk(nc, *args, out)
    r = run_bass_kernel_spmd(nc, [arrays], core_ids=[0])
    return r.results[0]["rows_out"][None]
```

```python
from contextlib import ExitStack

import concourse.bass as bass
import numpy as np
from concourse import mybir

P = 128
D_MODEL = 1024
SEQ = 1024
DEPTH = 2
HEAD = 64
CHUNK = 64
SWA_HEADS = 8
FOX_HEADS = 8
SWA_KV = 2
EPS = 1e-6
SCALE = HEAD ** -0.5
KT = D_MODEL // P
NB = SEQ // P
HALF = 512
TILES = 8
SWA_TILES = 4
FRESH = 1 + TILES - SWA_TILES
SLOTS = 8
SETS = 3
MASKED = 1e30
FSPLIT = 32
KSTEPS = 4

F32 = mybir.dt.float32
F32R = mybir.dt.float32r
BF16 = mybir.dt.bfloat16
ACT = mybir.ActivationFunctionType
ALU = mybir.AluOpType

CHUNKS = [("K", 0), ("Q", 0), ("V", 0)]
for _t in range(TILES):
    if _t >= SWA_TILES:
        CHUNKS += [("K", _t), ("V", _t)]
    CHUNKS += [("Q", _t + 1)] * (_t + 1 < TILES) + [("G", _t)]
CHUNKS += [("O", j) for j in range(2 * KT)]
NCH = len(CHUNKS)
AT = {key: n for n, key in enumerate(CHUNKS)}
KQ = [c for c in CHUNKS if c[0] in "KQ"]


def fill_steps(t):
    blocks = range(KT)
    steps = [("G", t, h, k) for h in range(2) for k in blocks]
    if t + 1 < TILES:
        return [("Q", t + 1, h, k) for h in range(2) for k in blocks] + steps
    return steps + [None] * KSTEPS + [("O", 0, 0, k) for k in blocks] + [
        ("O", 1, 0, k) for k in range(KSTEPS)]


def finished_fills(t, slot):
    return [s[:3] for s in fill_steps(t)[KSTEPS * slot:KSTEPS * (slot + 1)] if s and s[3] == KT - 1]


def split_slots(slot):
    return {4: [(t, 0) for t in range(4)], 5: [(t, 0) for t in range(4, 7)],
            6: [(7, 0)] + [(t, 1) for t in range(4)], 7: [(t, 1) for t in range(4, 7)]}.get(slot, [])


class Step:

    def __init__(self, turns, products):
        self.turns, self.products = turns, products
        self.width = P * len(turns)


class Unit:

    def __init__(self, layer, tile, slot):
        self.layer, self.tile, self.slot = layer, tile, slot
        self.m, self.head = divmod(slot, 2)
        self.place = tile * SLOTS + slot
        self.index = layer * TILES * SLOTS + self.place
        self.fox = tile >= SWA_TILES
        self.rows = slice(HEAD * self.head, HEAD * self.head + HEAD)
        self.other_rows = slice(HEAD - HEAD * self.head, P - HEAD * self.head)
        m = self.m
        if self.fox:
            self.steps = [Step([(0, 2 * i * P), (1, 2 * i * P), (0, (2 * i + 1) * P),
                                (1, (2 * i + 1) * P)],
                               [(2 * i, 0, 2 * P, 0), (2 * i + 1, 2 * P, 2 * P, 0)])
                          for i in range(m)]
            self.steps.append(Step([(0, 2 * m * P), (1, 2 * m * P), (1, (2 * m + 1) * P)],
                                   [(2 * m, 0, 2 * P, 0), (2 * m + 1, 2 * P, P, P)]))
        elif m:
            self.steps = [Step([(0, P), (1, 0), (1, P), (0, 0)],
                               [(2 * m, 0, 2 * P, 0), (2 * m + 1, 2 * P, P, P),
                                (2 * m - 1, 3 * P, P, 0)])]
        else:
            self.steps = [Step([(0, 0), (1, 0), (1, P)], [(0, 0, 2 * P, 0), (1, 2 * P, P, P)])]

    def width(self, a):
        qb = 2 * self.m + a
        return P * (qb + 1) if self.fox else (2 * P if qb else P)

    def key0(self, a):
        return 0 if self.fox else max(2 * self.m + a - 1, 0) * P

    def set_slot(self, a):
        return 2 * (self.place % SETS) + a


class Plan:

    def __init__(self):
        self.fill, self.use, self.units, self.turned = {}, {}, {}, {}
        self.scores_by_tile, self.steps_by_tile = {}, {}
        self.scores = self.steps = 0
        for layer in range(DEPTH):
            if not layer:
                self.turn(*[("norm", 0, i, g) for i in range(4) for g in range(2)])
            self.fills(layer, ("K", 0, 0))
            self.turn(*[("norm", layer, i, g) for i in (4, 5) for g in range(2)])
            self.fills(layer, ("Q", 0, 0))
            self.turn(*[("norm", layer, i, g) for i in (6, 7) for g in range(2)])
            self.fills(layer, ("F", 0, 0), ("K", 0, 1), ("F", 0, 1), ("Q", 0, 1), ("V", 0, 0),
                       ("V", 0, 1))
            self.turn(("V", layer, 0, 0), ("V", layer, 0, 1))
            pending = []
            for t in range(TILES):
                if t >= SWA_TILES:
                    for h in range(2):
                        self.finish(pending.pop(0))
                        self.fills(layer, ("K", t, h))
                    self.fills(layer, ("V", t, 0), ("V", t, 1))
                    self.turn(("V", layer, t, 0), ("V", layer, t, 1))
                for slot in range(SLOTS):
                    u = Unit(layer, t, slot)
                    self.units[layer, t, slot] = u
                    if len(pending) == 2:
                        self.finish(pending.pop(0))
                    u.score_chunks = [[], []]
                    for a in range(2):
                        for c0 in range(0, u.width(a), HALF):
                            u.score_chunks[a].append((self.scores, c0, min(HALF, u.width(a) - c0)))
                            self.scores += 1
                    u.chunk_order = [(a, j) for a in range(2) for j in range(len(u.score_chunks[a]))]
                    pending.append(u)
                self.fills(layer, *dict.fromkeys(s[:3] for s in fill_steps(t) if s))
                self.scores_by_tile[layer, t] = self.scores
            self.finish(pending.pop(0))
            self.turn(("O", layer, 0))
            self.finish(pending.pop(0))
            self.turned[layer] = self.uses_now()
            for j in range(2, 2 * KT):
                self.fills(layer, ("O", j, 0))
                self.turn(("O", layer, j - 1))
                if layer + 1 < DEPTH and j in NORM_TURN_AT:
                    self.turn(*[("norm", layer + 1, NORM_TURN_AT[j], g) for g in range(2)])
            self.turn(("O", layer, 2 * KT - 1))

    def uses_now(self):
        return len(self.use) + self.steps

    def turn(self, *keys):
        for key in keys:
            self.use[key] = self.uses_now()

    def fills(self, layer, *keys):
        for key in keys:
            self.fill[(layer,) + key] = len(self.fill)

    def finish(self, u):
        for step in u.steps:
            step.use = self.uses_now()
            step.index = self.steps
            self.steps += 1
        self.steps_by_tile[u.layer, u.tile] = self.steps


NORM_TURN_AT = {10: 0, 11: 1, 14: 2, 15: 3}
PIECE_AT = {8: ("scale", 0), 9: ("add", 0), 10: ("norm", 0),
            12: ("scale", 2), 13: ("add", 2), 14: ("norm", 2)}


def norm_order():
    order = [("norm", 0, i) for i in range(NB)]
    for layer in range(DEPTH):
        for i in range(0, NB, 2):
            order += [("out", layer, i), ("out", layer, i + 1)]
            if layer + 1 < DEPTH:
                order += [("norm", layer + 1, i), ("norm", layer + 1, i + 1)]
    return order


def hybrid_trunk(nc, x, w_chunks, w_gates, b_f, sinks, g_pre, g_post, rotary, ident_in, causal_in,
                 window_in, out):
    plan = Plan()
    norm_at = {key: n for n, key in enumerate(norm_order())}
    with ExitStack() as ctx:
        def sb(name, shape, dt=F32):
            return ctx.enter_context(nc.sbuf_tensor(name, shape, dt))

        def bank(name, n=1):
            return ctx.enter_context(nc.psum_tensor(name, [P, n * HALF], F32))

        def sem(name):
            return ctx.enter_context(nc.semaphore(name))

        trunk = nc.dram_tensor("trunk", [DEPTH - 1, SEQ, D_MODEL], F32).ap()
        c_dram = nc.dram_tensor("c_dram", [DEPTH, FOX_HEADS, SEQ], F32).ap()

        act_hi = sb("act_hi", [P, KT, SEQ], F32R)
        act_lo = sb("act_lo", [P, KT, SEQ], F32R)
        mixed = sb("mixed", [P, KT, SEQ])
        w_raw = sb("w_raw", [P, 2, KT, P])
        w_hi = sb("w_hi", [P, 2, KT, P], F32R)
        w_lo = sb("w_lo", [P, 2, KT, P], F32R)
        f_raw = sb("f_raw", [P, KT, FOX_HEADS])
        f_w = sb("f_w", [P, KT, FSPLIT + FOX_HEADS], F32R)
        q_hi = sb("q_hi", [P, 2, SEQ], F32R)
        q_lo = sb("q_lo", [P, 2, SEQ], F32R)
        k_hi = sb("k_hi", [P, SEQ], F32R)
        k_lo = sb("k_lo", [P, SEQ], F32R)
        v_sb = sb("v_sb", [P, NB, 4 * HEAD], F32R)
        prob = sb("prob", [P, 2 * SETS, SEQ])
        x_row = [prob[:, i] for i in range(4)]
        gain_pre, gain_post = prob[:, 4], prob[:, 5]
        forget = [mixed[0:FOX_HEADS, TILES - 1], mixed[0:FOX_HEADS, TILES - 2]]
        pt_hi = sb("pt_hi", [P, 2, HALF], F32R)
        pt_lo = sb("pt_lo", [P, 2, HALF], F32R)
        posb = sb("posb", [P, 2, SEQ])
        rope = sb("rope", [P, 2, HALF])
        stage = sb("stage", [P, HALF])
        o_tmp = sb("o_tmp", [P, 2 * P])
        ident = sb("ident", [P, P])
        ident_bf = sb("ident_bf", [P, P], BF16)
        causal = sb("causal", [P, P], BF16)
        window = sb("window", [P, 2 * P])
        sink_c = sb("sink_c", [P, DEPTH, SWA_HEADS])
        bf_c = sb("bf_c", [FOX_HEADS, DEPTH])
        half_c = sb("half_c", [P, 1])
        peak = sb("peak", [P, 2 * SETS, 2])
        nmax = sb("nmax", [P, 2 * SETS])
        rsum = sb("rsum", [P, 2 * SETS])
        esink = sb("esink", [P, 2 * SETS])
        rden = sb("rden", [P, 2 * SETS])
        stat = sb("stat", [P, len(norm_at), 3])

        proj = [bank(f"proj{i}") for i in range(2)]
        score_banks = bank("score", 2)
        score = [score_banks[:, i * HALF:(i + 1) * HALF] for i in range(2)]
        turn = [bank(f"turn{i}") for i in range(2)]
        mix = [bank(f"mix{i}") for i in range(2)]

        consts_loaded = sem("consts_loaded")
        consts_set = sem("consts_set")
        masks_set = sem("masks_set")
        pre_loaded = sem("pre_loaded")
        post_loaded = sem("post_loaded")
        x_loaded = [sem(f"x_loaded{i}") for i in range(4)]
        x_stored = [sem(f"x_stored{i}") for i in range(4)]
        posb_loaded = sem("posb_loaded")
        w_loaded = [sem(f"w_loaded{i}") for i in range(2)]
        f_loaded = sem("f_loaded")
        w_hi_pool = sem("w_hi_pool")
        w_hi_act = sem("w_hi_act")
        w_split = sem("w_split")
        f_hi_done = sem("f_hi_done")
        f_split = sem("f_split")
        squared = sem("squared")
        ms_ready = sem("ms_ready")
        rstd_ready = sem("rstd_ready")
        xn_ready = sem("xn_ready")
        y_scaled = sem("y_scaled")
        x_ready = sem("x_ready")
        h_hi = sem("h_hi")
        proj_done = sem("proj_done")
        proj_free = sem("proj_free")
        kq_hi = sem("kq_hi")
        rope_swapped = sem("rope_swapped")
        rope_mul = sem("rope_mul")
        rope_sum = sem("rope_sum")
        v_hi = sem("v_hi")
        tanh_done = sem("tanh_done")
        z_ready = sem("z_ready")
        e_ready = sem("e_ready")
        c_step = sem("c_step")
        c_summed = sem("c_summed")
        c_stored = sem("c_stored")
        turn_done = sem("turn_done")
        turn_free = sem("turn_free")
        score_done = sem("score_done")
        score_free = sem("score_free")
        nmax_ready = sem("nmax_ready")
        exp_done = sem("exp_done")
        sink_done = sem("sink_done")
        den_ready = sem("den_ready")
        rden_ready = sem("rden_ready")
        prob_ready = sem("prob_ready")
        pt_hi_done = sem("pt_hi_done")
        pv_done = sem("pv_done")
        o_copied = sem("o_copied")
        o_summed = sem("o_summed")
        gated = sem("gated")
        y_hi_done = sem("y_hi_done")
        y_ready = sem("y_ready")

        N_CONST = 5
        SCAN = [1 << j for j in range(10)]
        assert SCAN[-1] * 2 == SEQ
        N_C = 3
        SCAN_END = len(SCAN) % 2
        N_POSB = 16 * (1 + 2 * (TILES - SWA_TILES))

        def filled(layer, kind, t, h=0):
            return plan.fill[layer, kind, t, h] + 1

        def number(layer, chunk):
            return layer * NCH + AT[chunk]

        def used(g):
            layer, n = divmod(g, NCH)
            kind, t = CHUNKS[n]
            return filled(layer, kind, t, 0 if kind == "O" else 1)

        def rounded_by_act(g):
            layer, n = divmod(g, NCH)
            return n >= AT["O", 4] or (layer and n < 2)

        def rounded_before(g):
            return sum(rounded_by_act(i) == rounded_by_act(g) for i in range(g))

        kq_rank = {key: n for n, key in enumerate(
            sorted((k for k in plan.fill if k[1] in "KQ"), key=plan.fill.get))}
        rotations = [k for k in kq_rank if k[2] < SWA_TILES]
        last_turn = {u.index: u.steps[-1].use + 1 for u in plan.units.values()}

        def norm_at_layer(layer, i):
            return layer * NB + i + 1

        split_order = [key for slot in range(SLOTS) for key in split_slots(slot)] + [(TILES - 1, 1)]

        def split_rank(layer, t, h):
            return layer * 2 * TILES + split_order.index((t, h))

        def values_of(layer, t):
            return layer * FRESH + (0 if t < SWA_TILES else t - SWA_TILES + 1)

        def x_count(phase, i):
            return 16 * (2 * phase + i // 4 + 1)

        def head_of(t, head):
            return t + SWA_TILES * head

        def gate_place(t, h):
            return rope[:, 0] if (t, h) == (TILES - 1, 0) else stage[:]

        def gate_order(layer, t, h):
            return 2 * (layer * TILES + t) + h

        block = ctx.enter_context(nc.Block())

        @block.sync
        def _(sp):
            def broadcast(dst, row, n, done):
                sp.dma_start(dst, row.broadcast_to([P, n])).then_inc(done, 16)

            def weights(layer, n):
                g = layer * NCH + n
                if g >= 2:
                    sp.wait_ge(w_split, g - 1)
                sp.dma_start(w_raw[:, g % 2], w_chunks[layer, n]).then_inc(w_loaded[g % 2], 16)

            def load_rows(layer, i):
                src = trunk[layer - 1] if layer else x
                sp.dma_start(x_row[i % 4], src[i * P:(i + 1) * P]).then_inc(x_loaded[i % 4], 16)

            def residual_rows(layer, i):
                if i >= 4:
                    sp.wait_ge(x_stored[i % 4], 16 * (2 * layer + 1))
                    if layer + 1 < DEPTH:
                        sp.wait_ge(xn_ready, norm_at_layer(layer + 1, i - 4))
                load_rows(layer, i)

            def store_rows(layer, i):
                sp.wait_ge(x_ready, layer * NB + i + 1)
                dst = trunk[layer] if layer + 1 < DEPTH else out
                sp.dma_start(dst[i * P:(i + 1) * P], x_row[i % 4]).then_inc(x_stored[i % 4], 16)

            load_rows(0, 0)
            load_rows(0, 1)
            sp.dma_start(ident[:], ident_in).then_inc(consts_loaded, 16)
            broadcast(gain_pre, g_pre[0:1], D_MODEL, pre_loaded)
            load_rows(0, 2)
            load_rows(0, 3)
            weights(0, 0)
            sp.dma_start(posb[:], rotary).then_inc(posb_loaded, 16)
            sp.dma_start(stage[:, 0:P], causal_in).then_inc(consts_loaded, 16)
            sp.dma_start(window[:], window_in).then_inc(consts_loaded, 16)
            sp.dma_start(sink_c[:], sinks.rearrange("(o l) h -> o l h", o=1).broadcast_to(
                [P, DEPTH, SWA_HEADS])).then_inc(consts_loaded, 16)
            sp.dma_start(bf_c[:], b_f).then_inc(consts_loaded, 16)
            sp.dma_start(f_raw[:], w_gates[0]).then_inc(f_loaded, 16)
            weights(0, 1)
            for i in range(4, NB):
                sp.wait_ge(xn_ready, i - 3)
                load_rows(0, i)
            weights(0, 2)
            weights(0, 3)
            for layer in range(DEPTH):
                more = layer + 1 < DEPTH
                for n in range(4, NCH):
                    if n == AT["K", SWA_TILES]:
                        sp.wait_ge(c_summed, (layer + 1) * len(SCAN))
                        sp.dma_start(c_dram[layer], forget[SCAN_END]).then_inc(c_stored, 16)
                        if more:
                            sp.wait_ge(f_split, layer + 1)
                            sp.dma_start(f_raw[:], w_gates[layer + 1]).then_inc(f_loaded, 16)
                    for t in range(SWA_TILES, TILES):
                        if n == AT["K", t] + 3:
                            sp.wait_ge(c_stored, 16 * (layer + 1))
                            sp.wait_ge(score_free, plan.scores_by_tile[layer, t - 1])
                            for h in range(2):
                                j = 2 * (t - SWA_TILES) + h
                                broadcast(posb[:, h], c_dram[layer, j:j + 1], SEQ, posb_loaded)
                    if n == AT["O", 5]:
                        sp.wait_ge(turn_done, plan.turned[layer])
                        for i in range(4):
                            residual_rows(layer, i)
                        broadcast(gain_post, g_post[layer:layer + 1], D_MODEL, post_loaded)
                        if more:
                            broadcast(gain_pre, g_pre[layer + 1:layer + 2], D_MODEL, pre_loaded)
                            sp.dma_start(posb[:], rotary).then_inc(posb_loaded, 16)
                    weights(layer, n)
                if more:
                    weights(layer + 1, 0)
                for i in (0, 1):
                    store_rows(layer, i)
                if more:
                    weights(layer + 1, 1)
                for i in (4, 5):
                    residual_rows(layer, i)
                for i in (2, 3):
                    store_rows(layer, i)
                if more:
                    weights(layer + 1, 2)
                for i in (6, 7):
                    residual_rows(layer, i)
                if more:
                    weights(layer + 1, 3)
                for i in range(4, NB):
                    store_rows(layer, i)
            for i in range(4):
                sp.wait_ge(x_stored[i], 16 * 2 * DEPTH)

        @block.gpsimd
        def _(pool):
            pool.memset(half_c[:], -0.5).then_inc(consts_set, 1)
            pool.memset(f_w[:].bitcast(F32), 0.0).then_inc(consts_set, 1)
            pool.wait_ge(consts_set, 2)

            def gate_weights(layer):
                pool.wait_ge(f_loaded, 16 * (layer + 1))
                if layer:
                    pool.wait_ge(proj_done, filled(layer - 1, "F", 0, 1))
                pool.tensor_copy(f_w[:, :, 0:FOX_HEADS], f_raw[:]).then_inc(f_hi_done, 1)
                pool.wait_ge(f_hi_done, layer + 1)
                pool.tensor_tensor(f_w[:, :, FSPLIT:FSPLIT + FOX_HEADS], f_raw[:],
                                   f_w[:, :, 0:FOX_HEADS].bitcast(F32),
                                   ALU.subtract).then_inc(f_split, 1)

            def split(g):
                s = g % 2
                pool.wait_ge(w_loaded[s], 16 * (g // 2 + 1))
                if g >= 2:
                    pool.wait_ge(proj_done, used(g - 2))
                if rounded_by_act(g):
                    pool.wait_ge(w_hi_act, rounded_before(g) + 1)
                else:
                    pool.tensor_copy(w_hi[:, s], w_raw[:, s]).then_inc(w_hi_pool, 1)
                    pool.wait_ge(w_hi_pool, rounded_before(g) + 1)
                pool.tensor_tensor(w_lo[:, s], w_raw[:, s], w_hi[:, s].bitcast(F32),
                                   ALU.subtract).then_inc(w_split, 1)

            def forget_sums(layer, j0, j1):
                for j in range(j0, j1):
                    d = SCAN[j]
                    src, dst = forget[j % 2], forget[1 - j % 2]
                    if j == 0:
                        pool.wait_ge(c_step, (layer + 1) * N_C)
                    else:
                        pool.wait_ge(c_summed, layer * len(SCAN) + j)
                    pool.tensor_copy(dst[:, 0:d], src[:, 0:d])
                    pool.tensor_tensor(dst[:, d:SEQ], src[:, d:SEQ], src[:, 0:SEQ - d],
                                       ALU.add).then_inc(c_summed, 1)

            def rstd(kind, layer, i):
                for n in (norm_at[kind, layer, i], norm_at[kind, layer, i + 1]):
                    pool.wait_ge(ms_ready, n + 1)
                    pool.tensor_tensor(stat[:, n, 2:3], stat[:, n, 1:2], half_c[:],
                                       ALU.pow).then_inc(rstd_ready, 1)

            rstd("norm", 0, 0)
            split(0)
            rstd("norm", 0, 2)
            rstd("norm", 0, 4)
            split(1)
            rstd("norm", 0, 6)
            gate_weights(0)
            for layer in range(DEPTH):
                more = layer + 1 < DEPTH
                for n in range(2, AT["O", 0]):
                    split(layer * NCH + n)
                    if 0 <= n - AT["Q", 1] < 5:
                        forget_sums(layer, 2 * (n - AT["Q", 1]), 2 * (n - AT["Q", 1]) + 2)
                    if n == AT["Q", 5] and more:
                        gate_weights(layer + 1)
                split(layer * NCH + AT["O", 0])
                split(layer * NCH + AT["O", 1])
                for j in range(2 * KT):
                    g = layer * NCH + AT["O", j] + 2
                    if g < DEPTH * NCH:
                        split(g)
                    kind, i = PIECE_AT.get(j, ("", 0))
                    if kind == "scale":
                        rstd("out", layer, i)
                    if kind == "norm" and more:
                        rstd("norm", layer + 1, i)
                for i in (4, 6):
                    rstd("out", layer, i)
                    if more:
                        rstd("norm", layer + 1, i)

        @block.tensor
        def _(pe):
            def take_turn_bank(use):
                if use >= 2:
                    pe.wait_ge(turn_free, use - 1)
                return turn[use % 2]

            def four_turns(use, src):
                b = take_turn_bank(use)
                for j in range(4):
                    mm = nc.tensor.transpose(b[:, j * P:(j + 1) * P], src[:, j * P:(j + 1) * P],
                                             ident[:])
                mm.then_inc(turn_done, 1)

            def norm_turns(layer, i):
                pe.wait_ge(xn_ready, norm_at_layer(layer, i))
                for g in range(2):
                    four_turns(plan.use["norm", layer, i, g], mixed[:, i, g * HALF:(g + 1) * HALF])

            def value_turns(layer, t, h):
                pe.wait_ge(proj_free, filled(layer, "V", t, h))
                four_turns(plan.use["V", layer, t, h], stage)

            def new_values(layer, t):
                project(layer, "V", t, 0)
                project(layer, "V", t, 1, 0, 4)
                value_turns(layer, t, 0)
                project(layer, "V", t, 1, 4, KT)

            def out_turns(layer, j):
                pe.wait_ge(proj_free, filled(layer, "O", j))
                four_turns(plan.use["O", layer, j], rope[:, j % 2])

            def take_proj_bank(n):
                if n >= 2:
                    pe.wait_ge(proj_free, n - 1)
                return proj[n % 2]

            def forget_logits(layer, h):
                pe.wait_ge(f_split, layer + 1)
                pe.wait_ge(turn_free, plan.use["norm", layer, 4 * h + 3, 1] + 1)
                b = take_proj_bank(plan.fill[layer, "F", 0, h])
                cols = slice(h * HALF, (h + 1) * HALF)
                for k in range(KT):
                    nc.tensor.matmul(b[0:FSPLIT + FOX_HEADS, :], f_w[:, k, :],
                                     act_hi[:, k, cols], start=(k == 0), stop=False,
                                     skip_group_check=True)
                for k in range(KT):
                    mm = nc.tensor.matmul(b[0:FOX_HEADS, :], f_w[:, k, 0:FOX_HEADS],
                                          act_lo[:, k, cols], start=False, stop=(k == KT - 1),
                                          skip_group_check=True)
                mm.then_inc(proj_done, 1)

            def project(layer, kind, t, h, k0=0, k1=KT):
                g = number(layer, (kind, t))
                s = g % 2
                n = plan.fill[layer, kind, t, h]
                half = t // KT if kind == "O" else h
                cols = slice(half * HALF, (half + 1) * HALF)
                if k0 == 0:
                    pe.wait_ge(w_split, g + 1)
                    if kind != "O":
                        pe.wait_ge(turn_free, plan.use["norm", layer, 4 * h + 3, 1] + 1)
                    take_proj_bank(n)
                b = proj[n % 2]
                for k in range(k0, k1):
                    if kind == "O":
                        pe.wait_ge(y_ready, split_rank(layer, k, half) + 1)
                    nc.tensor.matmul(b[:], w_hi[:, s, k], act_hi[:, k, cols],
                                     start=(k == 0), stop=False)
                    nc.tensor.matmul(b[:], w_hi[:, s, k], act_lo[:, k, cols],
                                     start=False, stop=False)
                    mm = nc.tensor.matmul(b[:], w_lo[:, s, k], act_hi[:, k, cols],
                                          start=False, stop=(k == KT - 1))
                if k1 == KT:
                    mm.then_inc(proj_done, 1)

            def scores(u, i0, i1):
                q = u.tile % 2
                if u.slot == 0 and i0 == 0:
                    pe.wait_ge(proj_free, filled(u.layer, "Q", u.tile, 1))
                    if u.fox:
                        pe.wait_ge(proj_free, filled(u.layer, "K", u.tile, 1))
                for a, j in u.chunk_order[i0:i1]:
                    qb = 2 * u.m + a
                    qc = slice(qb * P, (qb + 1) * P)
                    index, c0, n = u.score_chunks[a][j]
                    if index >= 2:
                        pe.wait_ge(score_free, index - 1)
                    b = score[index % 2]
                    kc = slice(u.key0(a) + c0, u.key0(a) + c0 + n)
                    diagonal = u.fox and c0 + n == u.width(a)
                    nc.tensor.matmul(b[:, 0:n], q_hi[u.rows, q, qc], k_hi[u.rows, kc],
                                     start=True, stop=False, skip_group_check=True)
                    nc.tensor.matmul(b[:, 0:n], q_hi[u.rows, q, qc], k_lo[u.rows, kc],
                                     start=False, stop=False, skip_group_check=True)
                    mm = nc.tensor.matmul(b[:, 0:n], q_lo[u.rows, q, qc], k_hi[u.rows, kc],
                                          start=False, stop=not diagonal, skip_group_check=True)
                    if diagonal:
                        mm = nc.tensor.matmul(b[:, n - P:n], ident_bf[:], causal[:],
                                              start=False, stop=True, skip_group_check=True)
                    mm.then_inc(score_done, 1)

            def turn_probs(u, i):
                if i == 0:
                    pe.wait_ge(prob_ready, 2 * u.index + 2)
                if i < len(u.steps):
                    step = u.steps[i]
                    b = take_turn_bank(step.use)
                    for j, (a, col) in enumerate(step.turns):
                        mm = nc.tensor.transpose(b[:, j * P:(j + 1) * P],
                                                 prob[:, u.set_slot(a), col:col + P], ident[:])
                    mm.then_inc(turn_done, 1)

            def multiply_values(u, i):
                o, step = mix[u.index % 2], u.steps[i]
                first, last = i == 0, i == len(u.steps) - 1
                if first and u.index >= 2:
                    pe.wait_ge(o_summed, u.index - 1)
                if first and u.slot == 0:
                    t = u.tile if u.fox else 0
                    pe.wait_ge(turn_free, plan.use["V", u.layer, t, 1] + 1)
                pe.wait_ge(turn_free, step.use + 1)
                s = step.index % 2
                vc = slice(2 * HEAD * u.head, 2 * HEAD * (u.head + 1))
                for j, (kb, col, n, oc) in enumerate(step.products):
                    nc.tensor.matmul(o[:, oc:oc + n], v_sb[:, kb, vc], pt_hi[:, s, col:col + n],
                                     start=(first and j == 0), stop=False, skip_group_check=True)
                    mm = nc.tensor.matmul(o[:, oc:oc + n], v_sb[:, kb, vc], pt_lo[:, s, col:col + n],
                                          start=False, stop=(last and j == len(step.products) - 1),
                                          skip_group_check=True)
                mm.then_inc(pv_done, 1)

            def start_unit(u):
                turn_probs(u, 0)
                turn_probs(u, 1)

            def finish_step(u, i):
                multiply_values(u, i)
                turn_probs(u, i + 2)

            def finish_unit(u):
                for i in range(len(u.steps)):
                    finish_step(u, i)

            def slot_fill(layer, t, slot, i0, i1):
                for i in range(i0, i1):
                    if KSTEPS * slot + i < len(fill_steps(t)):
                        step = fill_steps(t)[KSTEPS * slot + i]
                        if step:
                            kind, tt, h, k = step
                            project(layer, kind, tt, h, k, k + 1)

            pe.wait_ge(masks_set, 2)
            for layer in range(DEPTH):
                if not layer:
                    for i in range(4):
                        norm_turns(layer, i)
                project(layer, "K", 0, 0)
                norm_turns(layer, 4)
                norm_turns(layer, 5)
                project(layer, "Q", 0, 0)
                norm_turns(layer, 6)
                norm_turns(layer, 7)
                forget_logits(layer, 0)
                project(layer, "K", 0, 1)
                forget_logits(layer, 1)
                project(layer, "Q", 0, 1)
                new_values(layer, 0)
                pending = []
                for t in range(TILES):
                    if t >= SWA_TILES:
                        for h in range(2):
                            start_unit(pending[0])
                            project(layer, "K", t, h)
                            finish_unit(pending.pop(0))
                        new_values(layer, t)
                    for slot in range(SLOTS):
                        u = plan.units[layer, t, slot]
                        old = pending.pop(0) if len(pending) == 2 else None
                        if old:
                            start_unit(old)
                        scores(u, 0, 2)
                        if slot == 0 and plan.use.get(("V", layer, t, 1)):
                            value_turns(layer, t, 1)
                        n = len(old.steps) if old else 0
                        cuts = {0: [0], 1: [0, 3], 2: [0, 2, 3], 3: [0, 1, 2, 3],
                                4: [0, 1, 2, 3, 3]}[n]
                        for i in range(max(n, 2)):
                            if i < n:
                                slot_fill(layer, t, slot, cuts[i], cuts[i + 1])
                                finish_step(old, i)
                            scores(u, 2 + i, 3 + i)
                        slot_fill(layer, t, slot, cuts[-1], KSTEPS)
                        pending.append(u)
                start_unit(pending[0])
                project(layer, "O", 1, 0, KSTEPS, KT)
                finish_unit(pending.pop(0))
                out_turns(layer, 0)
                start_unit(pending[0])
                project(layer, "O", 2, 0)
                finish_unit(pending.pop(0))
                for j in range(2, 2 * KT):
                    if j > 2:
                        project(layer, "O", j, 0)
                    out_turns(layer, j - 1)
                    if layer + 1 < DEPTH and j in NORM_TURN_AT:
                        norm_turns(layer + 1, NORM_TURN_AT[j])
                out_turns(layer, 2 * KT - 1)

        @block.scalar
        def _(act):
            act.wait_ge(masks_set, 2)

            def square(kind, layer, i):
                for r in (i, i + 1):
                    n = norm_at[kind, layer, r]
                    if kind == "norm" and layer:
                        act.wait_ge(x_ready, (layer - 1) * NB + r + 1)
                    elif kind == "norm":
                        act.wait_ge(x_loaded[r % 4], x_count(0, r))
                    else:
                        last = 2 * KT - 1 if r >= 4 else KT - 1
                        act.wait_ge(turn_free, plan.use["O", layer, last] + 1)
                    if n:
                        act.wait_ge(squared, n)
                    src = x_row[r % 4] if kind == "norm" else mixed[:, r]
                    nc.scalar.activation(score_banks[:], src, ACT.Square,
                                         accum_out=stat[:, n, 0:1]).then_inc(squared, 1)

            def norm_hi(layer, i):
                for g in range(2):
                    use = plan.use["norm", layer, i, g]
                    act.wait_ge(turn_done, use + 1)
                    nc.scalar.activation(act_hi[:, 4 * g:4 * g + 4, i * P:(i + 1) * P],
                                         turn[use % 2][:].rearrange("p (k s) -> p k s", k=4),
                                         ACT.Copy).then_inc(h_hi, 1)

            def forget_exps(layer):
                act.wait_ge(z_ready, 2 * (layer + 1))
                nc.scalar.activation(forget[1], forget[1], ACT.Exp).then_inc(e_ready, 1)
                act.wait_ge(e_ready, 2 * layer + 1)
                nc.scalar.activation(forget[1], forget[1], ACT.Ln, bias=1.0).then_inc(e_ready, 1)

            def swap_halves(layer, kind, t, h):
                n = rotations.index((layer, kind, t, h))
                act.wait_ge(proj_done, filled(layer, kind, t, h))
                if kind == "K" and h == 0 and layer:
                    act.wait_ge(turn_done, plan.use["O", layer - 1, 2 * KT - 1] + 1)
                if n:
                    act.wait_ge(rope_sum, n)
                b = proj[plan.fill[layer, kind, t, h] % 2]
                for q in range(4):
                    mv = nc.scalar.activation(rope[32 * q:32 * q + 32, 1],
                                              b[32 * (q ^ 1):32 * (q ^ 1) + 32, :], ACT.Copy)
                mv.then_inc(rope_swapped, 1)

            def round_half(layer, kind, t, h):
                cols = slice(h * HALF, (h + 1) * HALF)
                dst = k_hi[:, cols] if kind == "K" else q_hi[:, t % 2, cols]
                old = t - 1 if kind == "K" else t - 2
                if old >= 0:
                    act.wait_ge(score_done, plan.scores_by_tile[layer, old])
                elif layer:
                    act.wait_ge(score_done, plan.scores_by_tile[layer - 1, TILES - 1])
                if t < SWA_TILES:
                    swap_halves(layer, kind, t, h)
                    act.wait_ge(rope_sum, rotations.index((layer, kind, t, h)) + 1)
                    src = rope[:, 0]
                else:
                    act.wait_ge(proj_done, filled(layer, kind, t, h))
                    src = proj[plan.fill[layer, kind, t, h] % 2][:]
                nc.scalar.activation(dst, src, ACT.Copy,
                                     scale=SCALE if kind == "Q" else 1.0).then_inc(kq_hi, 1)

            def gate_tanh(layer, t, h):
                act.wait_ge(proj_done, filled(layer, "G", t, h))
                if h and t < TILES - 1:
                    act.wait_ge(gated, gate_order(layer, t, 0) + 1)
                elif t == 0 or t >= SWA_TILES:
                    act.wait_ge(turn_done, plan.use["V", layer, t, 1] + 1)
                else:
                    act.wait_ge(gated, gate_order(layer, t - 1, 1) + 1)
                if (t, h) == (TILES - 1, 0):
                    act.wait_ge(proj_free, filled(*[k for k in rotations if k[0] == layer][-1]))
                nc.scalar.activation(gate_place(t, h), proj[plan.fill[layer, "G", t, h] % 2][:], ACT.Tanh,
                                     scale=0.5).then_inc(tanh_done, 1)

            def value_hi(layer, t, h):
                use = plan.use["V", layer, t, h]
                act.wait_ge(turn_done, use + 1)
                if h == 0 and (layer or t):
                    act.wait_ge(pv_done, plan.steps_by_tile[(layer, t - 1) if t else
                                                            (layer - 1, TILES - 1)])
                b = turn[use % 2][:].rearrange("p (s d) -> p s d", s=4)
                kbs = slice(4 * h, 4 * h + 4)
                nc.scalar.activation(v_sb[:, kbs, 0:HEAD], b[:, :, 0:HEAD], ACT.Copy)
                nc.scalar.activation(v_sb[:, kbs, 3 * HEAD:4 * HEAD], b[:, :, HEAD:P],
                                     ACT.Copy).then_inc(v_hi, 1)

            def exponentials(u):
                for a in range(2):
                    n, s = 2 * u.index + a, u.set_slot(a)
                    act.wait_ge(nmax_ready, n + 1)
                    row = prob[:, s, 0:u.width(a)]
                    nc.scalar.activation(row, row, ACT.Exp, bias=nmax[:, s:s + 1],
                                         accum_out=rsum[:, s:s + 1]).then_inc(exp_done, 1)
                    if not u.fox:
                        h = head_of(u.tile, u.head)
                        nc.scalar.activation(esink[:, s:s + 1], sink_c[:, u.layer, h:h + 1],
                                             ACT.Exp, bias=nmax[:, s:s + 1]).then_inc(sink_done, 1)

            def probs_hi(u, i0, i1):
                for step in u.steps[i0:i1]:
                    act.wait_ge(turn_done, step.use + 1)
                    if step.index >= 2:
                        act.wait_ge(pv_done, step.index - 1)
                    nc.scalar.activation(pt_hi[:, step.index % 2, 0:step.width],
                                         turn[step.use % 2][:, 0:step.width],
                                         ACT.Copy).then_inc(pt_hi_done, 1)

            def copy_output(u):
                act.wait_ge(pv_done, u.steps[-1].index + 1)
                if u.index >= 2:
                    act.wait_ge(o_summed, u.index - 1)
                nc.scalar.activation(o_tmp[u.rows], mix[u.index % 2][u.other_rows, 0:2 * P],
                                     ACT.Copy).then_inc(o_copied, 1)

            def mixed_hi(layer, t, h):
                act.wait_ge(gated, gate_order(layer, t, h) + 1)
                act.wait_ge(proj_done, filled(layer, "G", TILES - 1, 1))
                cols = slice(h * HALF, (h + 1) * HALF)
                nc.scalar.activation(act_hi[:, t, cols], mixed[:, t, cols],
                                     ACT.Copy).then_inc(y_hi_done, 1)

            def round_weights(g):
                s = g % 2
                act.wait_ge(w_loaded[s], 16 * (g // 2 + 1))
                act.wait_ge(proj_done, used(g - 2))
                nc.scalar.activation(w_hi[:, s], w_raw[:, s], ACT.Copy).then_inc(w_hi_act, 1)

            def fills_done(layer, t, slot):
                for kind, tt, h in finished_fills(t, slot):
                    if kind == "G":
                        gate_tanh(layer, tt, h)
                    elif kind != "O":
                        round_half(layer, kind, tt, h)

            for i in (0, 2):
                square("norm", 0, i)
                norm_hi(0, i)
                norm_hi(0, i + 1)
            for layer in range(DEPTH):
                more = layer + 1 < DEPTH
                for i in (4, 6):
                    if layer == 0:
                        square("norm", 0, i)
                    else:
                        square("out", layer - 1, i)
                        square("norm", layer, i)
                    norm_hi(layer, i)
                    norm_hi(layer, i + 1)
                    round_half(layer, "K" if i == 4 else "Q", 0, 0)
                round_half(layer, "K", 0, 1)
                forget_exps(layer)
                round_half(layer, "Q", 0, 1)
                value_hi(layer, 0, 0)
                pending = []
                for t in range(TILES):
                    if t >= SWA_TILES:
                        for h in range(2):
                            u = pending.pop(0)
                            probs_hi(u, 0, 2)
                            if h == 0:
                                exponentials(pending[0])
                            probs_hi(u, 2, 4)
                            round_half(layer, "K", t, h)
                            copy_output(u)
                        value_hi(layer, t, 0)
                    for slot in range(SLOTS):
                        old = pending.pop(0) if len(pending) == 2 else None
                        if old:
                            probs_hi(old, 0, 2)
                        if slot == 0 and plan.use.get(("V", layer, t, 1)):
                            value_hi(layer, t, 1)
                        if pending:
                            exponentials(pending[-1])
                        if old:
                            probs_hi(old, 2, 4)
                        if t == TILES - 1:
                            for ts, h in split_slots(slot):
                                mixed_hi(layer, ts, h)
                        fills_done(layer, t, slot)
                        if old:
                            copy_output(old)
                        pending.append(plan.units[layer, t, slot])
                probs_hi(pending[0], 0, 2)
                exponentials(pending[1])
                probs_hi(pending[0], 2, 4)
                copy_output(pending[0])
                probs_hi(pending[1], 0, 4)
                copy_output(pending[1])
                mixed_hi(layer, TILES - 1, 1)
                for j in range(2, 2 * KT):
                    g = layer * NCH + AT["O", j] + 2
                    if g < DEPTH * NCH:
                        round_weights(g)
                    kind, i = PIECE_AT.get(j, ("", 0))
                    if kind == "scale":
                        square("out", layer, i)
                    if kind == "norm" and more:
                        square("norm", layer + 1, i)
                    if more and j in NORM_TURN_AT:
                        norm_hi(layer + 1, NORM_TURN_AT[j])
            for i in (4, 6):
                square("out", DEPTH - 1, i)

        @block.vector
        def _(dve):
            dve.wait_ge(consts_loaded, 16 * N_CONST)
            nc.vector.tensor_copy(ident_bf[:], ident[:]).then_inc(masks_set, 1)
            nc.vector.tensor_copy(causal[:], stage[:, 0:P]).then_inc(masks_set, 1)

            def mean_squares(kind, layer, i):
                for n in (norm_at[kind, layer, i], norm_at[kind, layer, i + 1]):
                    dve.wait_ge(squared, n + 1)
                    nc.vector.tensor_scalar(stat[:, n, 1:2], stat[:, n, 0:1], 1.0 / D_MODEL, EPS,
                                            ALU.mult, ALU.add).then_inc(ms_ready, 1)

            def scale_rows(layer, i):
                mean_squares("out", layer, i)
                dve.wait_ge(post_loaded, 16 * (layer + 1))
                for r in (i, i + 1):
                    n = norm_at["out", layer, r]
                    dve.wait_ge(rstd_ready, n + 1)
                    nc.vector.scalar_tensor_tensor(mixed[:, r], mixed[:, r], stat[:, n, 2:3],
                                                   gain_post, ALU.mult, ALU.mult).then_inc(y_scaled, 1)

            def add_rows(layer, i):
                for r in (i, i + 1):
                    dve.wait_ge(x_loaded[r % 4], x_count(1 + layer, r))
                    dve.wait_ge(y_scaled, layer * NB + r + 1)
                    nc.vector.tensor_tensor(x_row[r % 4], x_row[r % 4], mixed[:, r],
                                            ALU.add).then_inc(x_ready, 1)

            def norm_rows(layer, i):
                mean_squares("norm", layer, i)
                dve.wait_ge(pre_loaded, 16 * (layer + 1))
                for r in (i, i + 1):
                    n = norm_at["norm", layer, r]
                    dve.wait_ge(rstd_ready, n + 1)
                    if layer:
                        dve.wait_ge(x_ready, (layer - 1) * NB + r + 1)
                    nc.vector.scalar_tensor_tensor(mixed[:, r], x_row[r % 4], stat[:, n, 2:3],
                                                   gain_pre, ALU.mult, ALU.mult).then_inc(xn_ready, 1)

            def norm_lo(layer, i):
                rows = slice(i * P, (i + 1) * P)
                for g in range(2):
                    use = plan.use["norm", layer, i, g]
                    ks = slice(4 * g, 4 * g + 4)
                    dve.wait_ge(h_hi, 2 * (layer * NB + i) + g + 1)
                    nc.vector.tensor_tensor(act_lo[:, ks, rows],
                                            turn[use % 2][:].rearrange("p (k s) -> p k s", k=4),
                                            act_hi[:, ks, rows].bitcast(F32),
                                            ALU.subtract).then_inc(turn_free, 1)

            def forget_logits(layer, h):
                cols = slice(h * HALF, (h + 1) * HALF)
                z, minus = forget[0][:, cols], forget[1][:, cols]
                b = proj[plan.fill[layer, "F", 0, h] % 2]
                dve.wait_ge(proj_done, filled(layer, "F", 0, h))
                nc.vector.tensor_scalar(z, b[FSPLIT:FSPLIT + FOX_HEADS, :],
                                        bf_c[:, layer:layer + 1], None,
                                        ALU.add).then_inc(c_step, 1)
                dve.wait_ge(c_step, layer * N_C + h + 1)
                nc.vector.tensor_tensor(z, b[0:FOX_HEADS, :], z, ALU.add).then_inc(proj_free, 1)
                dve.wait_ge(proj_free, filled(layer, "F", 0, h))
                nc.vector.scalar_tensor_tensor(minus, z, -1.0, z, ALU.mult,
                                               ALU.min).then_inc(z_ready, 1)

            def forget_logs(layer):
                dve.wait_ge(e_ready, 2 * (layer + 1))
                nc.vector.scalar_tensor_tensor(forget[0], forget[0], 0.0, forget[1], ALU.min,
                                               ALU.subtract).then_inc(c_step, 1)

            def rotate(layer, kind, t, h):
                n = rotations.index((layer, kind, t, h))
                cols = slice(h * HALF, (h + 1) * HALF)
                b = proj[plan.fill[layer, kind, t, h] % 2]
                dve.wait_ge(proj_done, filled(layer, kind, t, h))
                dve.wait_ge(posb_loaded, layer * N_POSB + 16)
                if kind == "K" and h == 0 and layer:
                    dve.wait_ge(turn_done, plan.use["O", layer - 1, 2 * KT - 1] + 1)
                if n:
                    dve.wait_ge(proj_free, filled(*rotations[n - 1]))
                dve.wait_ge(rope_swapped, n + 1)
                nc.vector.tensor_tensor(rope[:, 0], b[:], posb[:, 0, cols],
                                        ALU.mult).then_inc(rope_mul, 1)
                nc.vector.tensor_tensor(rope[:, 1], rope[:, 1], posb[:, 1, cols],
                                        ALU.mult).then_inc(rope_mul, 1)
                dve.wait_ge(rope_mul, 2 * (n + 1))
                nc.vector.tensor_tensor(rope[:, 0], rope[:, 0], rope[:, 1],
                                        ALU.add).then_inc(rope_sum, 1)

            def split_half(layer, kind, t, h):
                cols = slice(h * HALF, (h + 1) * HALF)
                lo = k_lo[:, cols] if kind == "K" else q_lo[:, t % 2, cols]
                hi = k_hi[:, cols] if kind == "K" else q_hi[:, t % 2, cols]
                if t < SWA_TILES:
                    rotate(layer, kind, t, h)
                    src = rope[:, 0]
                else:
                    src = proj[plan.fill[layer, kind, t, h] % 2][:]
                dve.wait_ge(kq_hi, kq_rank[layer, kind, t, h] + 1)
                nc.vector.scalar_tensor_tensor(lo, src, SCALE if kind == "Q" else 1.0,
                                               hi.bitcast(F32), ALU.mult,
                                               ALU.subtract).then_inc(proj_free, 1)

            def gate_half(layer, t, h):
                dve.wait_ge(tanh_done, 2 * (layer * TILES + t) + h + 1)
                dst = gate_place(t, h)
                nc.vector.scalar_tensor_tensor(dst, dst, 1.0, proj[plan.fill[layer, "G", t, h] % 2][:],
                                               ALU.add, ALU.mult).then_inc(proj_free, 1)

            def gate_heads(layer, t, h):
                dve.wait_ge(proj_free, filled(layer, "G", t, h))
                dve.wait_ge(o_summed, (layer * TILES + t) * SLOTS + 4 * (h + 1))
                dst = mixed[:, t, h * HALF:(h + 1) * HALF]
                nc.vector.scalar_tensor_tensor(dst, gate_place(t, h), 0.5, dst, ALU.mult,
                                               ALU.mult).then_inc(gated, 1)

            def stage_values(layer, t, h):
                dve.wait_ge(proj_done, filled(layer, "V", t, h))
                if h:
                    dve.wait_ge(turn_done, plan.use["V", layer, t, 0] + 1)
                elif t or layer:
                    dve.wait_ge(gated, gate_order(layer, t, 0))
                nc.vector.tensor_copy(stage[:], proj[plan.fill[layer, "V", t, h] % 2][:]).then_inc(
                    proj_free, 1)

            def stage_outputs(layer, j):
                dve.wait_ge(proj_done, filled(layer, "O", j))
                if j >= 2:
                    dve.wait_ge(turn_done, plan.use["O", layer, j - 2] + 1)
                elif j == 0:
                    dve.wait_ge(proj_free, filled(layer, "Q", SWA_TILES - 1, 1))
                nc.vector.tensor_copy(rope[:, j % 2],
                                      proj[plan.fill[layer, "O", j, 0] % 2][:]).then_inc(proj_free, 1)

            def out_rows(layer, j):
                use = plan.use["O", layer, j]
                half, c = divmod(j, KT)
                dve.wait_ge(turn_done, use + 1)
                if j == 0:
                    dve.wait_ge(y_ready, split_rank(layer, 6, 1) + 1)
                if j == KT:
                    dve.wait_ge(y_ready, split_rank(layer, 7, 1) + 1)
                nc.vector.tensor_copy(mixed[:, 4 * half:4 * half + 4, c * P:(c + 1) * P],
                                      turn[use % 2][:].rearrange("p (s d) -> p s d", s=4)
                                      ).then_inc(turn_free, 1)

            def fills_done(layer, t, slot):
                for kind, tt, h in finished_fills(t, slot):
                    if kind == "G":
                        gate_half(layer, tt, h)
                    elif kind == "O":
                        stage_outputs(layer, tt)
                    else:
                        split_half(layer, kind, tt, h)

            def value_lo(layer, t, h):
                b = turn[plan.use["V", layer, t, h] % 2][:].rearrange("p (s d) -> p s d", s=4)
                kbs = slice(4 * h, 4 * h + 4)
                dve.wait_ge(v_hi, 2 * values_of(layer, t) + h + 1)
                nc.vector.tensor_tensor(v_sb[:, kbs, HEAD:2 * HEAD], b[:, :, 0:HEAD],
                                        v_sb[:, kbs, 0:HEAD].bitcast(F32), ALU.subtract)
                nc.vector.tensor_tensor(v_sb[:, kbs, 2 * HEAD:3 * HEAD], b[:, :, HEAD:P],
                                        v_sb[:, kbs, 3 * HEAD:4 * HEAD].bitcast(F32),
                                        ALU.subtract).then_inc(turn_free, 1)

            def bias_scores(u, i0, i1):
                if u.slot == 0 and i0 == 0:
                    if u.fox:
                        dve.wait_ge(posb_loaded,
                                    u.layer * N_POSB + 16 + 32 * (u.tile - SWA_TILES + 1))
                    elif u.tile == 0 and u.layer:
                        for i in range(4):
                            dve.wait_ge(x_stored[i], 16 * 2 * u.layer)
                if u.place >= SETS and i0 == 0:
                    dve.wait_ge(turn_done, last_turn[u.index - SETS])
                for a, j in u.chunk_order[i0:i1]:
                    s = u.set_slot(a)
                    index, c0, n = u.score_chunks[a][j]
                    dve.wait_ge(score_done, index + 1)
                    w0 = 2 * P - u.width(a)
                    bias = posb[:, u.head, c0:c0 + n] if u.fox else window[:, w0:w0 + n]
                    nc.vector.tensor_tensor_reduce(prob[:, s, c0:c0 + n], score[index % 2][:, 0:n],
                                                   bias, 1.0, -3e38, ALU.subtract, ALU.max,
                                                   peak[:, s, j:j + 1]).then_inc(score_free, 1)

            def row_maxima(u):
                for a in range(2):
                    s = u.set_slot(a)
                    dve.wait_ge(score_free, u.score_chunks[a][-1][0] + 1)
                    if not u.fox:
                        h = head_of(u.tile, u.head)
                        args = (sink_c[:, u.layer, h:h + 1], -1.0, ALU.max, ALU.mult)
                    elif len(u.score_chunks[a]) > 1:
                        args = (peak[:, s, 1:2], -1.0, ALU.max, ALU.mult)
                    else:
                        args = (-1.0, None, ALU.mult)
                    nc.vector.tensor_scalar(nmax[:, s:s + 1], peak[:, s, 0:1],
                                            *args).then_inc(nmax_ready, 1)

            def probs_lo(u, i0, i1):
                for step in u.steps[i0:i1]:
                    dve.wait_ge(pt_hi_done, step.index + 1)
                    s = step.index % 2
                    nc.vector.tensor_tensor(pt_lo[:, s, 0:step.width],
                                            turn[step.use % 2][:, 0:step.width],
                                            pt_hi[:, s, 0:step.width].bitcast(F32),
                                            ALU.subtract).then_inc(turn_free, 1)

            def denominators(u):
                for a in range(2):
                    n, s = 2 * u.index + a, u.set_slot(a)
                    dve.wait_ge(exp_done, n + 1)
                    if not u.fox:
                        count = 2 * ((u.layer * SWA_TILES + u.tile) * SLOTS + u.slot) + a + 1
                        dve.wait_ge(sink_done, count)
                        nc.vector.tensor_tensor(rsum[:, s:s + 1], rsum[:, s:s + 1],
                                                esink[:, s:s + 1], ALU.add).then_inc(den_ready, 1)
                        dve.wait_ge(den_ready, count)
                    nc.vector.reciprocal(rden[:, s:s + 1], rsum[:, s:s + 1]).then_inc(rden_ready, 1)

            def normalise(u):
                for a in range(2):
                    s = u.set_slot(a)
                    dve.wait_ge(rden_ready, 2 * u.index + a + 1)
                    row = prob[:, s, 0:u.width(a)]
                    nc.vector.tensor_scalar(row, row, rden[:, s:s + 1], None,
                                            ALU.mult).then_inc(prob_ready, 1)

            def sum_output(u):
                if u.tile == TILES - 2 and u.slot == 0:
                    dve.wait_ge(c_stored, 16 * (u.layer + 1))
                dve.wait_ge(o_copied, u.index + 1)
                nc.vector.tensor_tensor(mixed[u.rows, u.tile, 2 * P * u.m:2 * P * (u.m + 1)],
                                        mix[u.index % 2][u.rows, 0:2 * P],
                                        o_tmp[u.rows], ALU.add).then_inc(o_summed, 1)
                if u.slot % 4 == 3:
                    gate_heads(u.layer, u.tile, u.m // 2)

            def mixed_lo(layer, t, h):
                cols = slice(h * HALF, (h + 1) * HALF)
                dve.wait_ge(y_hi_done, split_rank(layer, t, h) + 1)
                nc.vector.tensor_tensor(act_lo[:, t, cols], mixed[:, t, cols],
                                        act_hi[:, t, cols].bitcast(F32),
                                        ALU.subtract).then_inc(y_ready, 1)

            for i in (0, 2):
                norm_rows(0, i)
                norm_lo(0, i)
                norm_lo(0, i + 1)
            for layer in range(DEPTH):
                more = layer + 1 < DEPTH
                for i in (4, 6):
                    if layer:
                        scale_rows(layer - 1, i)
                        add_rows(layer - 1, i)
                    norm_rows(layer, i)
                    norm_lo(layer, i)
                    norm_lo(layer, i + 1)
                    split_half(layer, "K" if i == 4 else "Q", 0, 0)
                forget_logits(layer, 0)
                split_half(layer, "K", 0, 1)
                forget_logits(layer, 1)
                split_half(layer, "Q", 0, 1)
                forget_logs(layer)
                stage_values(layer, 0, 0)
                value_lo(layer, 0, 0)
                stage_values(layer, 0, 1)
                pending = []
                for t in range(TILES):
                    if t >= SWA_TILES:
                        for h in range(2):
                            u = pending.pop(0)
                            probs_lo(u, 0, 2)
                            if h == 0:
                                denominators(pending[0])
                                normalise(pending[0])
                            probs_lo(u, 2, 4)
                            split_half(layer, "K", t, h)
                            sum_output(u)
                        stage_values(layer, t, 0)
                        value_lo(layer, t, 0)
                        stage_values(layer, t, 1)
                    for slot in range(SLOTS):
                        u = plan.units[layer, t, slot]
                        old = pending.pop(0) if len(pending) == 2 else None
                        if old:
                            probs_lo(old, 0, 2)
                        bias_scores(u, 0, 2)
                        if slot == 0 and plan.use.get(("V", layer, t, 1)):
                            value_lo(layer, t, 1)
                        if t == TILES - 1:
                            for ts, h in split_slots(slot):
                                mixed_lo(layer, ts, h)
                        if pending:
                            denominators(pending[-1])
                        if old:
                            probs_lo(old, 2, 3)
                        bias_scores(u, 2, 3)
                        if pending:
                            normalise(pending[-1])
                        if old:
                            probs_lo(old, 3, 4)
                        bias_scores(u, 3, 4)
                        row_maxima(u)
                        fills_done(layer, t, slot)
                        if old:
                            sum_output(old)
                        pending.append(u)
                probs_lo(pending[0], 0, 2)
                denominators(pending[1])
                normalise(pending[1])
                probs_lo(pending[0], 2, 4)
                stage_outputs(layer, 1)
                sum_output(pending[0])
                out_rows(layer, 0)
                probs_lo(pending[1], 0, 4)
                stage_outputs(layer, 2)
                sum_output(pending[1])
                mixed_lo(layer, TILES - 1, 1)
                out_rows(layer, 1)
                for j in range(3, 2 * KT):
                    stage_outputs(layer, j)
                    if more and j - 1 in NORM_TURN_AT:
                        norm_lo(layer + 1, NORM_TURN_AT[j - 1])
                    out_rows(layer, j - 1)
                    kind, i = PIECE_AT.get(j, ("", 0))
                    if kind == "scale":
                        scale_rows(layer, i)
                    if kind == "add":
                        add_rows(layer, i)
                    if kind == "norm" and more:
                        norm_rows(layer + 1, i)
                if more:
                    norm_lo(layer + 1, 3)
                out_rows(layer, 2 * KT - 1)
            for i in (4, 6):
                scale_rows(DEPTH - 1, i)
                add_rows(DEPTH - 1, i)


def w_in_columns():
    swa, kv, fox = SWA_HEADS * HEAD, SWA_KV * HEAD, FOX_HEADS * HEAD
    starts = np.cumsum([0, swa, kv, kv, swa, fox, fox, fox, FOX_HEADS])
    qa, ka, va, ga, qb, kb, vb, fb, gb = (int(s) for s in starts)

    def pair(base, a, b):
        return [base + HEAD * n + d for n in (a, b) for d in range(HEAD)]

    cols = []
    for kind, t in CHUNKS:
        if kind == "O":
            continue
        if t < SWA_TILES:
            base, heads = {"Q": (qa, (t, t + SWA_TILES)), "G": (ga, (t, t + SWA_TILES)),
                           "K": (ka, (0, 1)), "V": (va, (0, 1))}[kind]
        else:
            j = 2 * (t - SWA_TILES)
            base, heads = {"Q": qb, "K": kb, "V": vb, "G": gb}[kind], (j, j + 1)
        cols.append(pair(base, *heads))
    return cols, fb


def lay_out(w_in, w_out):
    cols, fb = w_in_columns()
    w = w_in.reshape(DEPTH, KT, P, -1)
    chunks = [w[..., c].transpose(0, 2, 1, 3) for c in cols]
    swa_rows = [HEAD * n + d for t in range(SWA_TILES) for n in (t, t + SWA_TILES) for d in range(HEAD)]
    rows = swa_rows + list(range(SWA_HEADS * HEAD, D_MODEL))
    wo = w_out[:, rows].reshape(DEPTH, KT, P, KT, P)
    chunks += 2 * [wo[:, :, :, c].transpose(0, 2, 1, 3) for c in range(KT)]
    gates = w[..., fb:fb + FOX_HEADS].transpose(0, 2, 1, 3)
    return np.ascontiguousarray(np.stack(chunks, axis=1)), np.ascontiguousarray(gates)


def constants():
    half = HEAD // 2
    freq = np.float32(10000.0) ** (-np.arange(half, dtype=np.float32) / np.float32(half))
    ang = np.arange(SEQ, dtype=np.float32)[:, None] * freq[None, :]
    cos, sin = np.cos(ang).T, np.sin(ang).T
    rotary = np.stack([np.concatenate([cos] * 4), np.concatenate([-sin, sin] * 2)], axis=1)
    q, k = np.arange(P)[:, None], np.arange(2 * P)[None, :]
    qc, kc = q // CHUNK, k // CHUNK - 2
    return {
        "rotary": rotary.astype(np.float32),
        "ident": np.eye(P, dtype=np.float32),
        "causal": np.where(k[:, :P] <= q, 0.0, -MASKED).astype(np.float32),
        "window": np.where((kc <= qc) & (kc > qc - 2), 0.0, MASKED).astype(np.float32),
    }


def kernel(x, w_in, b_f, sinks, w_out, g_pre, g_post):
    import concourse.bacc as bacc
    from concourse.bass_utils import run_bass_kernel_spmd

    nc = bacc.Bacc("TRN2", target_bir_lowering=False, num_devices=1)
    w_chunks, w_gates = lay_out(np.asarray(w_in), np.asarray(w_out))
    c = constants()
    arrays = {"x_in": np.ascontiguousarray(np.asarray(x)[0]), "w_chunks": w_chunks, "w_gates": w_gates,
              "b_f_in": np.ascontiguousarray(np.asarray(b_f).T), "sinks_in": np.ascontiguousarray(sinks),
              "g_pre_in": np.ascontiguousarray(g_pre), "g_post_in": np.ascontiguousarray(g_post),
              "rotary_in": c["rotary"], "ident_in": c["ident"],
              "causal_in": c["causal"], "window_in": c["window"]}
    args = [nc.dram_tensor(name, a.shape, mybir.dt.from_np(a.dtype), kind="ExternalInput").ap()
            for name, a in arrays.items()]
    out = nc.dram_tensor("rows_out", (SEQ, D_MODEL), F32, kind="ExternalOutput").ap()
    hybrid_trunk(nc, *args, out)
    r = run_bass_kernel_spmd(nc, [arrays], core_ids=[0])
    return r.results[0]["rows_out"][None]
```

```python
from contextlib import ExitStack

import concourse.bass as bass
import numpy as np
from concourse import mybir

P = 128
D_MODEL = 1024
SEQ = 1024
DEPTH = 2
HEAD = 64
CHUNK = 64
SWA_HEADS = 8
FOX_HEADS = 8
SWA_KV = 2
EPS = 1e-6
SCALE = HEAD ** -0.5
KT = D_MODEL // P
NB = SEQ // P
HALF = 512
TILES = 8
SWA_TILES = 4
FRESH = 1 + TILES - SWA_TILES
SLOTS = 8
SETS = 3
MASKED = 1e30
FSPLIT = 32
HEAD_ROWS = [slice(0, HEAD), slice(HEAD, P)]
KSTEPS = 4
STARTED = KT - 1

F32 = mybir.dt.float32
F32R = mybir.dt.float32r
BF16 = mybir.dt.bfloat16
ACT = mybir.ActivationFunctionType
ALU = mybir.AluOpType

CHUNKS = [("K", 0), ("Q", 0), ("V", 0)]
for _t in range(TILES):
    if _t >= SWA_TILES:
        CHUNKS += [("K", _t), ("V", _t)]
    CHUNKS += [("Q", _t + 1)] * (_t + 1 < TILES) + [("G", _t)]
CHUNKS += [("O", j) for j in range(2 * KT)]
NCH = len(CHUNKS)
AT = {key: n for n, key in enumerate(CHUNKS)}


def fill_steps(t):
    blocks = range(KT)
    steps = [("G", t, h, k) for h in range(2) for k in blocks]
    if t + 1 < TILES:
        return [("Q", t + 1, h, k) for h in range(2) for k in blocks] + steps
    first = [("O", 0, 0, k) for k in blocks]
    second = [("O", 1, 0, k) for k in range(STARTED)]
    return steps + first[:-1] + second[:5] + first[-1:] + second[5:]


def finished_fills(t, slot):
    return [s[:3] for s in fill_steps(t)[KSTEPS * slot:KSTEPS * (slot + 1)] if s and s[3] == KT - 1]


def split_slots(slot):
    return {2: [(0, 0), (1, 0)], 3: [(2, 0), (3, 0), (4, 0)], 4: [(5, 0), (6, 0)],
            6: [(7, 0)]}.get(slot, [])


class Step:

    def __init__(self, turns, products):
        self.turns, self.products = turns, products
        self.width = P * len(turns)


class Unit:

    def __init__(self, layer, tile, slot):
        self.layer, self.tile, self.slot = layer, tile, slot
        self.m, self.head = divmod(slot, 2)
        self.place = tile * SLOTS + slot
        self.index = layer * TILES * SLOTS + self.place
        self.fox = tile >= SWA_TILES
        self.rows, self.other_rows = HEAD_ROWS[self.head], HEAD_ROWS[1 - self.head]
        m = self.m
        if self.fox:
            self.steps = [Step([(0, 2 * i * P), (1, 2 * i * P), (0, (2 * i + 1) * P),
                                (1, (2 * i + 1) * P)],
                               [(2 * i, 0, 2 * P, 0), (2 * i + 1, 2 * P, 2 * P, 0)])
                          for i in range(m)]
            self.steps.append(Step([(0, 2 * m * P), (1, 2 * m * P), (1, (2 * m + 1) * P)],
                                   [(2 * m, 0, 2 * P, 0), (2 * m + 1, 2 * P, P, P)]))
        elif m:
            self.steps = [Step([(0, P), (1, 0), (1, P), (0, 0)],
                               [(2 * m, 0, 2 * P, 0), (2 * m + 1, 2 * P, P, P),
                                (2 * m - 1, 3 * P, P, 0)])]
        else:
            self.steps = [Step([(0, 0), (1, 0), (1, P)], [(0, 0, 2 * P, 0), (1, 2 * P, P, P)])]

    def width(self, a):
        qb = 2 * self.m + a
        return P * (qb + 1) if self.fox else (2 * P if qb else P)

    def key0(self, a):
        return 0 if self.fox else max(2 * self.m + a - 1, 0) * P

    def set_slot(self, a):
        return 2 * (self.place % SETS) + a


class Plan:

    def __init__(self):
        self.fill, self.use, self.units, self.turned = {}, {}, {}, {}
        self.scores_by_tile, self.steps_by_tile = {}, {}
        self.scores = self.steps = 0
        for layer in range(DEPTH):
            if not layer:
                self.turn(*[("norm", 0, i, g) for i in range(4) for g in range(2)])
            self.fills(layer, ("K", 0, 0))
            self.fills(layer, ("Q", 0, 0))
            self.turn(*[("norm", layer, i, g) for i in range(4, NB) for g in range(2)])
            self.fills(layer, ("K", 0, 1), ("V", 0, 0), ("Q", 0, 1), ("V", 0, 1))
            self.turn(("V", layer, 0, 0), ("V", layer, 0, 1))
            pending = []
            for t in range(TILES):
                if t >= SWA_TILES:
                    for h in range(2):
                        self.finish(pending.pop(0))
                        self.fills(layer, ("K", t, h))
                    self.fills(layer, ("V", t, 0), ("V", t, 1))
                    self.turn(("V", layer, t, 0), ("V", layer, t, 1))
                for slot in range(SLOTS):
                    u = Unit(layer, t, slot)
                    self.units[layer, t, slot] = u
                    if len(pending) == 2:
                        self.finish(pending.pop(0))
                    u.score_chunks = [[], []]
                    for a in range(2):
                        for c0 in range(0, u.width(a), HALF):
                            u.score_chunks[a].append((self.scores, c0, min(HALF, u.width(a) - c0)))
                            self.scores += 1
                    u.chunk_order = [(a, j) for a in range(2) for j in range(len(u.score_chunks[a]))]
                    pending.append(u)
                self.fills(layer, *dict.fromkeys(s[:3] for s in fill_steps(t) if s))
                self.scores_by_tile[layer, t] = self.scores
            self.finish(pending.pop(0))
            self.finish(pending.pop(0))
            self.turned[layer] = self.uses_now()
            self.turn(("O", layer, 0))
            for j in range(2, 2 * KT):
                self.fills(layer, ("O", j, 0))
                self.turn(("O", layer, j - 1))
                if layer + 1 < DEPTH and j in NORM_TURN_AT:
                    self.turn(*[("norm", layer + 1, NORM_TURN_AT[j], g) for g in range(2)])
            self.turn(("O", layer, 2 * KT - 1))

    def uses_now(self):
        return len(self.use) + self.steps

    def turn(self, *keys):
        for key in keys:
            self.use[key] = self.uses_now()

    def fills(self, layer, *keys):
        for key in keys:
            self.fill[(layer,) + key] = len(self.fill)

    def finish(self, u):
        for step in u.steps:
            step.use = self.uses_now()
            step.index = self.steps
            self.steps += 1
        self.steps_by_tile[u.layer, u.tile] = self.steps


SPLIT_AT = {2: [(0, 1), (1, 1)], 3: [(2, 1)], 4: [(3, 1)], 5: [(4, 1)], 6: [(5, 1)],
            7: [(6, 1), (7, 1)]}
NORM_TURN_AT = {12: 0, 13: 1, 14: 2, 15: 3}
ADD_AT = {8: 0, 9: 2}
SQUARE_AT = {9: 0, 10: 2}
NORM_AT = {10: 0, 11: 2}


def hybrid_trunk(nc, x, w_chunks, w_gates, b_f, sinks, g_pre, g_post, rotary, ident_in, causal_in,
                 window_in, out):
    plan = Plan()
    with ExitStack() as ctx:
        def sb(name, shape, dt=F32):
            return ctx.enter_context(nc.sbuf_tensor(name, shape, dt))

        def bank(name, n=1):
            return ctx.enter_context(nc.psum_tensor(name, [P, n * HALF], F32))

        def sem(name):
            return ctx.enter_context(nc.semaphore(name))

        trunk = nc.dram_tensor("trunk", [DEPTH - 1, SEQ, D_MODEL], F32).ap()
        c_dram = nc.dram_tensor("c_dram", [DEPTH, FOX_HEADS, SEQ], F32).ap()

        act_hi = sb("act_hi", [P, KT, SEQ], F32R)
        act_lo = sb("act_lo", [P, KT, SEQ], F32R)
        mixed = sb("mixed", [P, KT, SEQ])
        w_raw = sb("w_raw", [P, 2, KT, P])
        w_hi = sb("w_hi", [P, 2, KT, P], F32R)
        w_lo = sb("w_lo", [P, 2, KT, P], F32R)
        f_raw = sb("f_raw", [P, KT, FOX_HEADS])
        f_w = sb("f_w", [P, KT, FSPLIT + FOX_HEADS], F32R)
        q_both = sb("q_both", [P, 2, 2, SEQ], F32R)
        k_hi = sb("k_hi", [P, 2, SEQ], F32R)
        k_lo = sb("k_lo", [P, SEQ], F32R)
        v_sb = sb("v_sb", [P, NB, 4 * HEAD], F32R)
        prob = sb("prob", [P, 2 * SETS, SEQ])
        x_row = [prob[:, i] for i in (0, 1, 4, 5)]
        gain_pre, gain_post = prob[:, 2], prob[:, 3]
        forget = [mixed[0:FOX_HEADS, TILES - 1], mixed[0:FOX_HEADS, TILES - 2]]
        pt_hi = sb("pt_hi", [P, 2, HALF], F32R)
        pt_lo = sb("pt_lo", [P, 2, HALF], F32R)
        posb = sb("posb", [P, 2, SEQ])
        rope = sb("rope", [P, 2, HALF])
        stage = sb("stage", [P, HALF])
        o_tmp = sb("o_tmp", [P, 2 * P])
        ident = sb("ident", [P, P])
        ident_bf = sb("ident_bf", [P, P], BF16)
        causal = sb("causal", [P, P], BF16)
        window = sb("window", [P, 2 * P])
        sink_c = sb("sink_c", [P, DEPTH, SWA_HEADS])
        bf_c = sb("bf_c", [FOX_HEADS, DEPTH])
        half_c = sb("half_c", [P, 4])
        peak = sb("peak", [P, 2 * SETS, 2])
        nmax = sb("nmax", [P, 2 * SETS])
        rsum = sb("rsum", [P, 2 * SETS])
        esink = sb("esink", [P, 2 * SETS])
        rden = sb("rden", [P, 2 * SETS])
        stat = sb("stat", [P, DEPTH * NB, 3])
        out_sq = sb("out_sq", [P, NB, KT])
        out_stat = sb("out_stat", [P, 2 * DEPTH, 3, 4])

        proj = [bank(f"proj{i}") for i in range(2)]
        score_banks = bank("score", 2)
        score = [score_banks[:, i * HALF:(i + 1) * HALF] for i in range(2)]
        turn = [bank(f"turn{i}") for i in range(2)]
        mix = [bank(f"mix{i}") for i in range(2)]

        ident_loaded = sem("ident_loaded")
        consts_loaded = sem("consts_loaded")
        consts_set = sem("consts_set")
        masks_set = sem("masks_set")
        pre_loaded = sem("pre_loaded")
        post_loaded = sem("post_loaded")
        x_loaded = [sem(f"x_loaded{i}") for i in range(4)]
        x_stored = [sem(f"x_stored{i}") for i in range(4)]
        posb_loaded = sem("posb_loaded")
        w_loaded = [sem(f"w_loaded{i}") for i in range(2)]
        f_loaded = sem("f_loaded")
        w_hi_pool = sem("w_hi_pool")
        w_hi_act = sem("w_hi_act")
        w_split = sem("w_split")
        f_hi_done = sem("f_hi_done")
        f_split = sem("f_split")
        f_done = sem("f_done")
        squared = sem("squared")
        ms_ready = sem("ms_ready")
        rstd_ready = sem("rstd_ready")
        xn_ready = sem("xn_ready")
        out_squared = sem("out_squared")
        out_summed = sem("out_summed")
        out_ms_ready = sem("out_ms_ready")
        out_rstd_ready = sem("out_rstd_ready")
        x_ready = sem("x_ready")
        h_hi = sem("h_hi")
        proj_done = sem("proj_done")
        proj_free = sem("proj_free")
        kq_hi = sem("kq_hi")
        k_copied = sem("k_copied")
        rope_swapped = sem("rope_swapped")
        rope_mul = sem("rope_mul")
        rope_sum = sem("rope_sum")
        v_hi = sem("v_hi")
        tanh_done = sem("tanh_done")
        z_ready = sem("z_ready")
        e_ready = sem("e_ready")
        c_step = sem("c_step")
        c_summed = sem("c_summed")
        c_stored = sem("c_stored")
        turn_done = sem("turn_done")
        turn_free = sem("turn_free")
        score_done = sem("score_done")
        score_free = sem("score_free")
        nmax_ready = sem("nmax_ready")
        exp_done = sem("exp_done")
        sink_done = sem("sink_done")
        den_ready = sem("den_ready")
        rden_ready = sem("rden_ready")
        first_ready = sem("first_ready")
        prob_ready = sem("prob_ready")
        pt_hi_done = sem("pt_hi_done")
        pv_done = sem("pv_done")
        o_copied = sem("o_copied")
        o_summed = sem("o_summed")
        gated = sem("gated")
        y_hi_done = sem("y_hi_done")
        y_ready = sem("y_ready")

        N_CONST = 4
        SCAN = [1 << j for j in range(10)]
        assert SCAN[-1] * 2 == SEQ
        N_C = 5
        SCAN_END = len(SCAN) % 2
        SCAN_AT = {AT["Q", 1]: (0, 1), AT["Q", 2]: (1, 3), AT["G", 1]: (3, 4),
                   AT["Q", 3]: (4, 6), AT["G", 2]: (6, 7), AT["Q", 4]: (7, 10)}
        N_POSB = 16 * (1 + 2 * (TILES - SWA_TILES))

        def filled(layer, kind, t, h=0):
            return plan.fill[layer, kind, t, h] + 1

        def number(layer, chunk):
            return layer * NCH + AT[chunk]

        def used(g):
            layer, n = divmod(g, NCH)
            kind, t = CHUNKS[n]
            return filled(layer, kind, t, 0 if kind == "O" else 1)

        def rounded_by_act(g):
            layer, n = divmod(g, NCH)
            return n >= AT["O", 2] or n < 3

        def rounded_before(g):
            return sum(rounded_by_act(i) == rounded_by_act(g) for i in range(g))

        kq_rank = {key: n for n, key in enumerate(
            sorted((k for k in plan.fill if k[1] in "KQ"), key=plan.fill.get))}
        rotations = [k for k in kq_rank if k[2] < SWA_TILES]
        last_turn = {u.index: u.steps[-1].use + 1 for u in plan.units.values()}

        def norm_at_layer(layer, i):
            return layer * NB + i + 1

        split_order = [key for slot in range(SLOTS) for key in split_slots(slot)]
        split_order += [key for j in SPLIT_AT for key in SPLIT_AT[j]]

        def split_rank(layer, t, h):
            return layer * 2 * TILES + split_order.index((t, h))

        def gains_free(layer):
            return max(last_turn[u.index] for u in plan.units.values()
                       if u.layer == layer and u.set_slot(0) == 2)

        def values_of(layer, t):
            return layer * FRESH + (0 if t < SWA_TILES else t - SWA_TILES + 1)

        def x_count(phase, i):
            return 16 * (2 * phase + i // 4 + 1)

        def head_of(t, head):
            return t + SWA_TILES * head

        def probs_before(u, which=""):
            fox = u.layer * (TILES - SWA_TILES) * SLOTS + max(u.place - SWA_TILES * SLOTS, 0)
            return fox if which else 2 * u.index - fox

        def gate_place(t, h):
            return rope[:, 0] if (t, h) == (TILES - 1, 0) else stage[:]

        def gate_order(layer, t, h):
            return 2 * (layer * TILES + t) + h

        block = ctx.enter_context(nc.Block())

        @block.sync
        def _(sp):
            def broadcast(dst, row, n, done):
                sp.dma_start(dst, row.broadcast_to([P, n])).then_inc(done, 16)

            def weights(layer, n):
                g = layer * NCH + n
                if g >= 2:
                    sp.wait_ge(w_split, g - 1)
                sp.dma_start(w_raw[:, g % 2], w_chunks[layer, n]).then_inc(w_loaded[g % 2], 16)

            def load_rows(layer, i):
                src = trunk[layer - 1] if layer else x
                sp.dma_start(x_row[i % 4], src[i * P:(i + 1) * P]).then_inc(x_loaded[i % 4], 16)

            def residual_rows(layer, i):
                if i >= 4:
                    sp.wait_ge(x_stored[i % 4], 16 * (2 * layer + 1))
                    if layer + 1 < DEPTH:
                        sp.wait_ge(xn_ready, norm_at_layer(layer + 1, i - 4))
                load_rows(layer, i)

            def store_rows(layer, i):
                sp.wait_ge(x_ready, layer * NB + i + 1)
                dst = trunk[layer] if layer + 1 < DEPTH else out
                sp.dma_start(dst[i * P:(i + 1) * P], x_row[i % 4]).then_inc(x_stored[i % 4], 16)

            load_rows(0, 0)
            sp.dma_start(ident[:], ident_in).then_inc(ident_loaded, 16)
            load_rows(0, 1)
            broadcast(gain_pre, g_pre[0:1], D_MODEL, pre_loaded)
            load_rows(0, 2)
            load_rows(0, 3)
            weights(0, 0)
            sp.dma_start(posb[:], rotary).then_inc(posb_loaded, 16)
            sp.dma_start(stage[:, 0:P], causal_in).then_inc(consts_loaded, 16)
            sp.dma_start(window[:], window_in).then_inc(consts_loaded, 16)
            sp.dma_start(sink_c[:], sinks.rearrange("(o l) h -> o l h", o=1).broadcast_to(
                [P, DEPTH, SWA_HEADS])).then_inc(consts_loaded, 16)
            sp.dma_start(bf_c[:], b_f).then_inc(consts_loaded, 16)
            sp.dma_start(f_raw[:], w_gates[0]).then_inc(f_loaded, 16)
            weights(0, 1)
            for i in range(4, NB):
                sp.wait_ge(xn_ready, i - 3)
                load_rows(0, i)
            weights(0, 2)
            weights(0, 3)
            for layer in range(DEPTH):
                more = layer + 1 < DEPTH
                for n in range(4, NCH):
                    if n == AT["K", SWA_TILES]:
                        sp.wait_ge(c_summed, (layer + 1) * len(SCAN))
                        sp.dma_start(c_dram[layer], forget[SCAN_END]).then_inc(c_stored, 16)
                        if more:
                            sp.wait_ge(f_split, layer + 1)
                            sp.dma_start(f_raw[:], w_gates[layer + 1]).then_inc(f_loaded, 16)
                    for t in range(SWA_TILES, TILES):
                        if n == AT["K", t] + 3:
                            sp.wait_ge(c_stored, 16 * (layer + 1))
                            sp.wait_ge(score_free, plan.scores_by_tile[layer, t - 1])
                            for h in range(2):
                                j = 2 * (t - SWA_TILES) + h
                                broadcast(posb[:, h], c_dram[layer, j:j + 1], SEQ, posb_loaded)
                    if n == AT["O", 3]:
                        sp.wait_ge(turn_done, gains_free(layer))
                        broadcast(gain_post, g_post[layer:layer + 1], D_MODEL, post_loaded)
                        if more:
                            broadcast(gain_pre, g_pre[layer + 1:layer + 2], D_MODEL, pre_loaded)
                    if n == AT["O", 5]:
                        sp.wait_ge(turn_done, plan.turned[layer])
                        for i in range(4):
                            residual_rows(layer, i)
                        if more:
                            sp.dma_start(posb[:], rotary).then_inc(posb_loaded, 16)
                    if n == AT["O", 13]:
                        for i in range(4):
                            store_rows(layer, i)
                    weights(layer, n)
                for i in range(4, NB):
                    residual_rows(layer, i)
                if more:
                    for n in range(3):
                        weights(layer + 1, n)
                for i in range(4, NB):
                    store_rows(layer, i)
                if more:
                    weights(layer + 1, 3)
            for i in range(4):
                sp.wait_ge(x_stored[i], 16 * 2 * DEPTH)

        @block.gpsimd
        def _(pool):
            pool.memset(half_c[:], -0.5).then_inc(consts_set, 1)
            pool.memset(f_w[:].bitcast(F32), 0.0).then_inc(consts_set, 1)
            pool.wait_ge(consts_set, 2)

            def gate_weights(layer):
                pool.wait_ge(f_loaded, 16 * (layer + 1))
                if layer:
                    pool.wait_ge(f_done, 2 * layer)
                pool.tensor_copy(f_w[:, :, 0:FOX_HEADS], f_raw[:]).then_inc(f_hi_done, 1)
                pool.wait_ge(f_hi_done, layer + 1)
                pool.tensor_tensor(f_w[:, :, FSPLIT:FSPLIT + FOX_HEADS], f_raw[:],
                                   f_w[:, :, 0:FOX_HEADS].bitcast(F32),
                                   ALU.subtract).then_inc(f_split, 1)

            def split(g):
                s = g % 2
                pool.wait_ge(w_loaded[s], 16 * (g // 2 + 1))
                if g >= 2:
                    pool.wait_ge(proj_done, used(g - 2))
                if rounded_by_act(g):
                    pool.wait_ge(w_hi_act, rounded_before(g) + 1)
                else:
                    pool.tensor_copy(w_hi[:, s], w_raw[:, s]).then_inc(w_hi_pool, 1)
                    pool.wait_ge(w_hi_pool, rounded_before(g) + 1)
                pool.tensor_tensor(w_lo[:, s], w_raw[:, s], w_hi[:, s].bitcast(F32),
                                   ALU.subtract).then_inc(w_split, 1)

            def finish_rotation(layer, kind, t, h):
                n = rotations.index((layer, kind, t, h))
                cols = slice(h * HALF, (h + 1) * HALF)
                pool.wait_ge(posb_loaded, layer * N_POSB + 16)
                pool.wait_ge(rope_swapped, n + 1)
                pool.tensor_tensor(rope[:, 1], rope[:, 1], posb[:, 1, cols],
                                   ALU.mult).then_inc(rope_mul, 1)
                pool.wait_ge(rope_mul, 2 * (n + 1))
                pool.tensor_tensor(rope[:, 0], rope[:, 0], rope[:, 1],
                                   ALU.add).then_inc(rope_sum, 1)

            def forget_sums(layer, j0, j1):
                for j in range(j0, j1):
                    d = SCAN[j]
                    src, dst = forget[j % 2], forget[1 - j % 2]
                    if j == 0:
                        pool.wait_ge(c_step, (layer + 1) * N_C)
                    else:
                        pool.wait_ge(c_summed, layer * len(SCAN) + j)
                    pool.tensor_copy(dst[:, 0:d], src[:, 0:d])
                    pool.tensor_tensor(dst[:, d:SEQ], src[:, d:SEQ], src[:, 0:SEQ - d],
                                       ALU.add).then_inc(c_summed, 1)

            def rstd(layer, i):
                n = layer * NB + i
                pool.wait_ge(ms_ready, n // 2 + 1)
                pool.tensor_tensor(stat[:, n:n + 2, 2], stat[:, n:n + 2, 1], half_c[:, 0:2],
                                   ALU.pow).then_inc(rstd_ready, 1)

            def out_rstd(layer, half):
                n = 2 * layer + half
                pool.wait_ge(out_ms_ready, n + 1)
                pool.tensor_tensor(out_stat[:, n, 2], out_stat[:, n, 1], half_c[:],
                                   ALU.pow).then_inc(out_rstd_ready, 1)

            rstd(0, 0)
            rstd(0, 2)
            split(0)
            rstd(0, 4)
            split(1)
            rstd(0, 6)
            gate_weights(0)
            for layer in range(DEPTH):
                more = layer + 1 < DEPTH
                for n in range(2, AT["O", 0]):
                    for t in range(1, SWA_TILES):
                        if n == AT["Q", t + 1]:
                            finish_rotation(layer, "Q", t, 0)
                            finish_rotation(layer, "Q", t, 1)
                    split(layer * NCH + n)
                    if n in SCAN_AT:
                        forget_sums(layer, *SCAN_AT[n])
                    if n == AT["Q", 5] and more:
                        gate_weights(layer + 1)
                split(layer * NCH + AT["O", 0])
                split(layer * NCH + AT["O", 1])
                for j in range(2 * KT):
                    g = layer * NCH + AT["O", j] + 2
                    if j == KT:
                        out_rstd(layer, 0)
                    if j in NORM_AT and more:
                        rstd(layer + 1, NORM_AT[j])
                    if g < DEPTH * NCH:
                        split(g)
                out_rstd(layer, 1)
                for i in (4, 6):
                    if more:
                        rstd(layer + 1, i)

        @block.tensor
        def _(pe):
            def take_turn_bank(use):
                if use >= 2:
                    pe.wait_ge(turn_free, use - 1)
                return turn[use % 2]

            def four_turns(use, src):
                b = take_turn_bank(use)
                for j in range(4):
                    mm = nc.tensor.transpose(b[:, j * P:(j + 1) * P], src[:, j * P:(j + 1) * P],
                                             ident[:])
                mm.then_inc(turn_done, 1)

            def norm_turns(layer, i):
                pe.wait_ge(xn_ready, norm_at_layer(layer, i))
                for g in range(2):
                    four_turns(plan.use["norm", layer, i, g], mixed[:, i, g * HALF:(g + 1) * HALF])

            def value_turns(layer, t, h):
                pe.wait_ge(proj_free, filled(layer, "V", t, h))
                four_turns(plan.use["V", layer, t, h], stage)

            def second_values(layer, t):
                project(layer, "V", t, 1, 0, 4)
                value_turns(layer, t, 0)
                project(layer, "V", t, 1, 4, KT)

            def out_turns(layer, j):
                pe.wait_ge(proj_free, filled(layer, "O", j))
                four_turns(plan.use["O", layer, j], rope[:, j % 2])

            def take_proj_bank(n):
                if n >= 2:
                    pe.wait_ge(proj_free, n - 1)
                return proj[n % 2]

            def forget_logits(layer, h):
                pe.wait_ge(f_split, layer + 1)
                if layer and h == 0:
                    pe.wait_ge(out_squared, 2 * KT * layer)
                pe.wait_ge(turn_free, plan.use["norm", layer, 4 * h + 3, 1] + 1)
                b = score[h]
                cols = slice(h * HALF, (h + 1) * HALF)
                for k in range(KT):
                    nc.tensor.matmul(b[0:FSPLIT + FOX_HEADS, :], f_w[:, k, :],
                                     act_hi[:, k, cols], start=(k == 0), stop=False,
                                     skip_group_check=True)
                for k in range(KT):
                    mm = nc.tensor.matmul(b[0:FOX_HEADS, :], f_w[:, k, 0:FOX_HEADS],
                                          act_lo[:, k, cols], start=False, stop=(k == KT - 1),
                                          skip_group_check=True)
                mm.then_inc(f_done, 1)

            def project(layer, kind, t, h, k0=0, k1=KT):
                g = number(layer, (kind, t))
                s = g % 2
                n = plan.fill[layer, kind, t, h]
                half = t // KT if kind == "O" else h
                cols = slice(half * HALF, (half + 1) * HALF)
                if k0 == 0:
                    pe.wait_ge(w_split, g + 1)
                    if kind != "O":
                        pe.wait_ge(turn_free, plan.use["norm", layer, 4 * h + 3, 1] + 1)
                    take_proj_bank(n)
                b = proj[n % 2]
                for k in range(k0, k1):
                    if kind == "O":
                        pe.wait_ge(y_ready, split_rank(layer, k, half) + 1)
                    nc.tensor.matmul(b[:], w_hi[:, s, k], act_hi[:, k, cols],
                                     start=(k == 0), stop=False)
                    nc.tensor.matmul(b[:], w_hi[:, s, k], act_lo[:, k, cols],
                                     start=False, stop=False)
                    mm = nc.tensor.matmul(b[:], w_lo[:, s, k], act_hi[:, k, cols],
                                          start=False, stop=(k == KT - 1))
                if k1 == KT:
                    mm.then_inc(proj_done, 1)

            def scores(u, i0, i1):
                q = u.tile % 2
                if u.slot == 0 and i0 == 0:
                    pe.wait_ge(proj_free, filled(u.layer, "Q", u.tile, 1))
                    if u.fox:
                        pe.wait_ge(proj_free, filled(u.layer, "K", u.tile, 1))
                    pe.wait_ge(k_copied, 2 * (values_of(u.layer, u.tile) + 1))
                    if u.tile == 0:
                        pe.wait_ge(c_step, u.layer * N_C + 4)
                for a, j in u.chunk_order[i0:i1]:
                    qb = 2 * u.m + a
                    qc = slice(qb * P, (qb + 1) * P)
                    index, c0, n = u.score_chunks[a][j]
                    if index >= 2:
                        pe.wait_ge(score_free, index - 1)
                    b = score[index % 2]
                    kc = slice(u.key0(a) + c0, u.key0(a) + c0 + n)
                    diagonal = u.fox and c0 + n == u.width(a)
                    nc.tensor.matmul(b[:, 0:n], q_both[:, q, u.head, qc], k_hi[:, u.head, kc],
                                     start=True, stop=False, skip_group_check=True)
                    mm = nc.tensor.matmul(b[:, 0:n], q_both[u.rows, q, u.head, qc], k_lo[u.rows, kc],
                                          start=False, stop=not diagonal, skip_group_check=True)
                    if diagonal:
                        mm = nc.tensor.matmul(b[:, n - P:n], ident_bf[:], causal[:],
                                              start=False, stop=True, skip_group_check=True)
                    mm.then_inc(score_done, 1)

            def turn_probs(u, i):
                if i == 0:
                    pe.wait_ge(prob_ready, probs_before(u) + 2 - u.fox)
                    if u.fox:
                        pe.wait_ge(first_ready, probs_before(u, "first") + 1)
                if i < len(u.steps):
                    step = u.steps[i]
                    b = take_turn_bank(step.use)
                    for j, (a, col) in enumerate(step.turns):
                        mm = nc.tensor.transpose(b[:, j * P:(j + 1) * P],
                                                 prob[:, u.set_slot(a), col:col + P], ident[:])
                    mm.then_inc(turn_done, 1)

            def multiply_values(u, i):
                o, step = mix[u.index % 2], u.steps[i]
                first, last = i == 0, i == len(u.steps) - 1
                if first and u.index >= 2:
                    pe.wait_ge(o_summed, u.index - 1)
                if first and u.slot == 0:
                    t = u.tile if u.fox else 0
                    pe.wait_ge(turn_free, plan.use["V", u.layer, t, 1] + 1)
                pe.wait_ge(turn_free, step.use + 1)
                s = step.index % 2
                vc = slice(2 * HEAD * u.head, 2 * HEAD * (u.head + 1))
                for j, (kb, col, n, oc) in enumerate(step.products):
                    nc.tensor.matmul(o[:, oc:oc + n], v_sb[:, kb, vc], pt_hi[:, s, col:col + n],
                                     start=(first and j == 0), stop=False, skip_group_check=True)
                    mm = nc.tensor.matmul(o[:, oc:oc + n], v_sb[:, kb, vc], pt_lo[:, s, col:col + n],
                                          start=False, stop=(last and j == len(step.products) - 1),
                                          skip_group_check=True)
                mm.then_inc(pv_done, 1)

            def start_unit(u):
                turn_probs(u, 0)
                turn_probs(u, 1)

            def finish_step(u, i):
                multiply_values(u, i)
                turn_probs(u, i + 2)

            def finish_beside(u, pieces):
                start_unit(u)
                for i in range(len(u.steps)):
                    if i < len(pieces):
                        project(u.layer, *pieces[i])
                    finish_step(u, i)
                for piece in pieces[len(u.steps):]:
                    project(u.layer, *piece)

            def slot_fill(layer, t, slot, i0, i1):
                for i in range(i0, i1):
                    if KSTEPS * slot + i < len(fill_steps(t)):
                        step = fill_steps(t)[KSTEPS * slot + i]
                        if step:
                            kind, tt, h, k = step
                            project(layer, kind, tt, h, k, k + 1)

            pe.wait_ge(ident_loaded, 16)
            for layer in range(DEPTH):
                if not layer:
                    for i in range(4):
                        norm_turns(layer, i)
                project(layer, "K", 0, 0, 0, 2)
                if layer:
                    out_turns(layer - 1, 2 * KT - 1)
                project(layer, "K", 0, 0, 2, KT)
                project(layer, "Q", 0, 0)
                forget_logits(layer, 0)
                norm_turns(layer, 4)
                norm_turns(layer, 5)
                norm_turns(layer, 6)
                norm_turns(layer, 7)
                project(layer, "K", 0, 1)
                forget_logits(layer, 1)
                project(layer, "V", 0, 0)
                project(layer, "Q", 0, 1)
                second_values(layer, 0)
                pe.wait_ge(masks_set, 2)
                pending = []
                for t in range(TILES):
                    if t >= SWA_TILES:
                        for h in range(2):
                            finish_beside(pending.pop(0), [("K", t, h, 0, 3), ("K", t, h, 3, 5),
                                                           ("K", t, h, 5, KT)])
                        project(layer, "V", t, 0)
                        second_values(layer, t)
                    for slot in range(SLOTS):
                        u = plan.units[layer, t, slot]
                        old = pending.pop(0) if len(pending) == 2 else None
                        if old:
                            start_unit(old)
                        scores(u, 0, 2)
                        if slot == 0 and plan.use.get(("V", layer, t, 1)):
                            value_turns(layer, t, 1)
                        n = len(old.steps) if old else 0
                        cuts = {0: [0], 1: [0, 3], 2: [0, 2, 3], 3: [0, 1, 2, 3],
                                4: [0, 1, 2, 3, 4]}[n]
                        for i in range(max(n, 2)):
                            if i < n:
                                slot_fill(layer, t, slot, cuts[i], cuts[i + 1])
                                finish_step(old, i)
                            scores(u, 2 + i, 3 + i)
                        slot_fill(layer, t, slot, cuts[-1], KSTEPS)
                        pending.append(u)
                finish_beside(pending.pop(0), [("O", 1, 0, STARTED, KT), ("O", 2, 0, 0, 1),
                                               ("O", 2, 0, 1, 3)])
                finish_beside(pending.pop(0), [("O", 2, 0, 3, 4), ("O", 2, 0, 4, 6),
                                               ("O", 2, 0, 6, KT)])
                out_turns(layer, 0)
                for j in range(2, 2 * KT):
                    if j > 2:
                        project(layer, "O", j, 0, 0, 2)
                    out_turns(layer, j - 1)
                    if j > 2:
                        project(layer, "O", j, 0, 2, 5)
                    if layer + 1 < DEPTH and j in NORM_TURN_AT:
                        norm_turns(layer + 1, NORM_TURN_AT[j])
                    if j > 2:
                        project(layer, "O", j, 0, 5, KT)
            out_turns(DEPTH - 1, 2 * KT - 1)

        @block.scalar
        def _(act):
            def square(layer, *rows):
                for r in rows:
                    n = layer * NB + r
                    if layer:
                        act.wait_ge(x_ready, (layer - 1) * NB + r + 1)
                    else:
                        act.wait_ge(x_loaded[r % 4], x_count(0, r))
                    if n:
                        act.wait_ge(squared, n)
                    nc.scalar.activation(pt_hi[:].rearrange("p a b -> p (a b)"),
                                         x_row[r % 4], ACT.Square,
                                         accum_out=stat[:, n, 0:1]).then_inc(squared, 1)

            def square_outputs(layer, j):
                use = plan.use["O", layer, j]
                half, c = divmod(j, KT)
                act.wait_ge(turn_done, use + 1)
                if j % KT == 0:
                    if layer:
                        act.wait_ge(out_summed, 2 * layer + half - 1)
                for s in range(4):
                    to = P * (4 * (j % 2) + s)
                    sq = nc.scalar.activation(score_banks[:, to:to + P],
                                              turn[use % 2][:, s * P:(s + 1) * P], ACT.Square,
                                              accum_out=out_sq[:, 4 * half + s, c:c + 1])
                sq.then_inc(out_squared, 1)

            def norm_hi(layer, i):
                for g in range(2):
                    use = plan.use["norm", layer, i, g]
                    act.wait_ge(turn_done, use + 1)
                    nc.scalar.activation(act_hi[:, 4 * g:4 * g + 4, i * P:(i + 1) * P],
                                         turn[use % 2][:].rearrange("p (k s) -> p k s", k=4),
                                         ACT.Copy).then_inc(h_hi, 1)

            def forget_exps(layer):
                act.wait_ge(z_ready, 2 * (layer + 1))
                nc.scalar.activation(forget[1], forget[1], ACT.Exp).then_inc(e_ready, 1)
                act.wait_ge(e_ready, 2 * layer + 1)
                nc.scalar.activation(forget[1], forget[1], ACT.Ln, bias=1.0).then_inc(e_ready, 1)

            def swap_halves(layer, kind, t, h):
                n = rotations.index((layer, kind, t, h))
                act.wait_ge(proj_done, filled(layer, kind, t, h))
                if kind == "K" and h == 0 and layer:
                    act.wait_ge(turn_done, plan.use["O", layer - 1, 2 * KT - 1] + 1)
                if n:
                    act.wait_ge(rope_sum, n)
                b = proj[plan.fill[layer, kind, t, h] % 2]
                for q in range(4):
                    mv = nc.scalar.activation(rope[32 * q:32 * q + 32, 1],
                                              b[32 * (q ^ 1):32 * (q ^ 1) + 32, :], ACT.Copy)
                mv.then_inc(rope_swapped, 1)

            def round_half(layer, kind, t, h):
                cols = slice(h * HALF, (h + 1) * HALF)
                old = t - 1 if kind == "K" else t - 2
                if old >= 0:
                    act.wait_ge(score_done, plan.scores_by_tile[layer, old])
                elif layer:
                    act.wait_ge(score_done, plan.scores_by_tile[layer - 1, TILES - 1])
                if t < SWA_TILES:
                    act.wait_ge(rope_sum, rotations.index((layer, kind, t, h)) + 1)
                    src = rope[:, 0]
                else:
                    act.wait_ge(proj_done, filled(layer, kind, t, h))
                    src = proj[plan.fill[layer, kind, t, h] % 2][:]
                for head, own in enumerate(HEAD_ROWS):
                    if kind == "Q":
                        hi = nc.scalar.activation(q_both[own, t % 2, head, cols], src[own],
                                                  ACT.Copy, scale=SCALE)
                    else:
                        hi = nc.scalar.activation(k_hi[own, head, cols], src[own], ACT.Copy)
                hi.then_inc(kq_hi, 1)
                if kind == "K":
                    act.wait_ge(kq_hi, kq_rank[layer, kind, t, h] + 1)
                    for head, own in enumerate(HEAD_ROWS):
                        copy = nc.scalar.activation(k_hi[HEAD_ROWS[1 - head], head, cols],
                                                    k_hi[own, head, cols].bitcast(F32), ACT.Copy)
                    copy.then_inc(k_copied, 1)

            def gate_tanh(layer, t, h):
                act.wait_ge(proj_done, filled(layer, "G", t, h))
                if h and t < TILES - 1:
                    act.wait_ge(gated, gate_order(layer, t, 0) + 1)
                elif t == 0 or t >= SWA_TILES:
                    act.wait_ge(turn_done, plan.use["V", layer, t, 1] + 1)
                else:
                    act.wait_ge(gated, gate_order(layer, t - 1, 1) + 1)
                if (t, h) == (TILES - 1, 0):
                    act.wait_ge(proj_free, filled(*[k for k in rotations if k[0] == layer][-1]))
                nc.scalar.activation(gate_place(t, h), proj[plan.fill[layer, "G", t, h] % 2][:], ACT.Tanh,
                                     scale=0.5).then_inc(tanh_done, 1)

            def value_hi(layer, t, h):
                use = plan.use["V", layer, t, h]
                act.wait_ge(turn_done, use + 1)
                if h == 0 and (layer or t):
                    act.wait_ge(pv_done, plan.steps_by_tile[(layer, t - 1) if t else
                                                            (layer - 1, TILES - 1)])
                b = turn[use % 2][:].rearrange("p (s d) -> p s d", s=4)
                kbs = slice(4 * h, 4 * h + 4)
                nc.scalar.activation(v_sb[:, kbs, 0:HEAD], b[:, :, 0:HEAD], ACT.Copy)
                nc.scalar.activation(v_sb[:, kbs, 3 * HEAD:4 * HEAD], b[:, :, HEAD:P],
                                     ACT.Copy).then_inc(v_hi, 1)

            def exponentials(u):
                for a in range(2):
                    n, s = 2 * u.index + a, u.set_slot(a)
                    act.wait_ge(nmax_ready, n + 1)
                    row = prob[:, s, 0:u.width(a)]
                    nc.scalar.activation(row, row, ACT.Exp, bias=nmax[:, s:s + 1],
                                         accum_out=rsum[:, s:s + 1]).then_inc(exp_done, 1)
                    if not u.fox:
                        h = head_of(u.tile, u.head)
                        nc.scalar.activation(esink[:, s:s + 1], sink_c[:, u.layer, h:h + 1],
                                             ACT.Exp, bias=nmax[:, s:s + 1]).then_inc(sink_done, 1)

            def normalise_first(u):
                if u.fox:
                    s = u.set_slot(0)
                    act.wait_ge(rden_ready, 2 * u.index + 1)
                    row = prob[:, s, 0:u.width(0)]
                    nc.scalar.activation(row, row, ACT.Copy,
                                         scale=rden[:, s:s + 1]).then_inc(first_ready, 1)

            def probs_hi(u, i0, i1):
                for step in u.steps[i0:i1]:
                    act.wait_ge(turn_done, step.use + 1)
                    if step.index >= 2:
                        act.wait_ge(pv_done, step.index - 1)
                    nc.scalar.activation(pt_hi[:, step.index % 2, 0:step.width],
                                         turn[step.use % 2][:, 0:step.width],
                                         ACT.Copy).then_inc(pt_hi_done, 1)

            def copy_output(u):
                act.wait_ge(pv_done, u.steps[-1].index + 1)
                if u.index >= 2:
                    act.wait_ge(o_summed, u.index - 1)
                nc.scalar.activation(o_tmp[u.rows], mix[u.index % 2][u.other_rows, 0:2 * P],
                                     ACT.Copy).then_inc(o_copied, 1)

            def mixed_hi(layer, t, h):
                act.wait_ge(gated, gate_order(layer, t, h) + 1)
                act.wait_ge(proj_done, filled(layer, "G", TILES - 1, h))
                cols = slice(h * HALF, (h + 1) * HALF)
                nc.scalar.activation(act_hi[:, t, cols], mixed[:, t, cols],
                                     ACT.Copy).then_inc(y_hi_done, 1)

            def round_weights(g):
                s = g % 2
                act.wait_ge(w_loaded[s], 16 * (g // 2 + 1))
                if g >= 2:
                    act.wait_ge(proj_done, used(g - 2))
                nc.scalar.activation(w_hi[:, s], w_raw[:, s], ACT.Copy).then_inc(w_hi_act, 1)

            def fills_done(layer, t, slot):
                for kind, tt, h in finished_fills(t, slot):
                    if kind == "G":
                        gate_tanh(layer, tt, h)
                    elif kind == "Q" and tt < SWA_TILES:
                        swap_halves(layer, kind, tt, h)
                    elif kind == "Q":
                        round_half(layer, kind, tt, h)

            def rotated_fills(layer, t, slot):
                for kind, tt, h in finished_fills(t, slot):
                    if kind == "Q" and tt < SWA_TILES:
                        round_half(layer, kind, tt, h)

            for layer in range(DEPTH):
                more = layer + 1 < DEPTH
                if layer == 0:
                    square(0, 0, 1, 2)
                    norm_hi(0, 0)
                    square(0, 3)
                    norm_hi(0, 1)
                    round_weights(0)
                    norm_hi(0, 2)
                    square(0, 4, 5)
                    norm_hi(0, 3)
                    round_weights(1)
                    square(0, 6, 7)
                    swap_halves(0, "K", 0, 0)
                else:
                    swap_halves(layer, "K", 0, 0)
                    square(layer, 4, 5, 6, 7)
                norm_hi(layer, 4)
                norm_hi(layer, 5)
                round_half(layer, "K", 0, 0)
                norm_hi(layer, 6)
                norm_hi(layer, 7)
                swap_halves(layer, "Q", 0, 0)
                round_half(layer, "Q", 0, 0)
                round_weights(number(layer, ("V", 0)))
                swap_halves(layer, "K", 0, 1)
                round_half(layer, "K", 0, 1)
                forget_exps(layer)
                swap_halves(layer, "Q", 0, 1)
                round_half(layer, "Q", 0, 1)
                value_hi(layer, 0, 0)
                pending = []
                for t in range(TILES):
                    if t >= SWA_TILES:
                        for h in range(2):
                            u = pending.pop(0)
                            probs_hi(u, 0, 2)
                            if h == 0:
                                exponentials(pending[0])
                                normalise_first(pending[0])
                            probs_hi(u, 2, 4)
                            round_half(layer, "K", t, h)
                            copy_output(u)
                        value_hi(layer, t, 0)
                    for slot in range(SLOTS):
                        old = pending.pop(0) if len(pending) == 2 else None
                        if old:
                            probs_hi(old, 0, 2)
                        if slot == 0 and plan.use.get(("V", layer, t, 1)):
                            value_hi(layer, t, 1)
                        if pending:
                            exponentials(pending[-1])
                        if (t, slot) == (TILES - 1, SLOTS - 1):
                            round_weights(number(layer, ("O", 2)))
                        if old:
                            probs_hi(old, 2, 3)
                        if pending:
                            normalise_first(pending[-1])
                        if old:
                            probs_hi(old, 3, 4)
                        if slot > 1:
                            rotated_fills(layer, t, slot - 2)
                        if old:
                            copy_output(old)
                        fills_done(layer, t, slot)
                        if t == TILES - 1:
                            for ts, h in split_slots(slot):
                                mixed_hi(layer, ts, h)
                        pending.append(plan.units[layer, t, slot])
                probs_hi(pending[0], 0, 2)
                exponentials(pending[1])
                normalise_first(pending[1])
                probs_hi(pending[0], 2, 4)
                copy_output(pending[0])
                round_weights(number(layer, ("O", 3)))
                probs_hi(pending[1], 0, 4)
                copy_output(pending[1])
                square_outputs(layer, 0)
                for j in range(2, 2 * KT):
                    for ts, h in SPLIT_AT.get(j, []):
                        mixed_hi(layer, ts, h)
                    square_outputs(layer, j - 1)
                    if more and j in NORM_TURN_AT:
                        norm_hi(layer + 1, NORM_TURN_AT[j])
                    g = layer * NCH + AT["O", j] + 2
                    if g < DEPTH * NCH:
                        round_weights(g)
                    if more and j in SQUARE_AT:
                        square(layer + 1, SQUARE_AT[j], SQUARE_AT[j] + 1)
                square_outputs(layer, 2 * KT - 1)

        @block.vector
        def _(dve):
            def set_masks():
                dve.wait_ge(ident_loaded, 16)
                dve.wait_ge(consts_loaded, 16 * N_CONST)
                nc.vector.tensor_copy(ident_bf[:], ident[:]).then_inc(masks_set, 1)
                nc.vector.tensor_copy(causal[:], stage[:, 0:P]).then_inc(masks_set, 1)

            def mean_squares(layer, i):
                n = layer * NB + i
                dve.wait_ge(squared, n + 2)
                nc.vector.tensor_scalar(stat[:, n:n + 2, 1], stat[:, n:n + 2, 0], 1.0 / D_MODEL, EPS,
                                        ALU.mult, ALU.add).then_inc(ms_ready, 1)

            def out_mean_squares(layer, half):
                n = 2 * layer + half
                dve.wait_ge(out_squared, (n + 1) * KT)
                nc.vector.tensor_reduce(out_stat[:, n, 0], out_sq[:, 4 * half:4 * half + 4],
                                        mybir.AxisListType.X, ALU.add).then_inc(out_summed, 1)
                dve.wait_ge(out_summed, n + 1)
                nc.vector.tensor_scalar(out_stat[:, n, 1], out_stat[:, n, 0], 1.0 / D_MODEL, EPS,
                                        ALU.mult, ALU.add).then_inc(out_ms_ready, 1)

            def add_rows(layer, i):
                n = 2 * layer + i // 4
                dve.wait_ge(out_rstd_ready, n + 1)
                dve.wait_ge(turn_free, plan.use["O", layer, KT * (i // 4 + 1) - 1] + 1)
                for r in (i, i + 1):
                    dve.wait_ge(x_loaded[r % 4], x_count(1 + layer, r))
                    nc.vector.scalar_tensor_tensor(x_row[r % 4], mixed[:, r],
                                                   out_stat[:, n, 2, r % 4:r % 4 + 1], x_row[r % 4],
                                                   ALU.mult, ALU.add).then_inc(x_ready, 1)

            def norm_rows(layer, i):
                dve.wait_ge(pre_loaded, 16 * (layer + 1))
                dve.wait_ge(rstd_ready, (layer * NB + i) // 2 + 1)
                for r in (i, i + 1):
                    n = layer * NB + r
                    if layer:
                        dve.wait_ge(x_ready, (layer - 1) * NB + r + 1)
                    nc.vector.scalar_tensor_tensor(mixed[:, r], x_row[r % 4], stat[:, n, 2:3],
                                                   gain_pre, ALU.mult, ALU.mult).then_inc(xn_ready, 1)

            def norm_lo(layer, i):
                rows = slice(i * P, (i + 1) * P)
                for g in range(2):
                    use = plan.use["norm", layer, i, g]
                    ks = slice(4 * g, 4 * g + 4)
                    dve.wait_ge(h_hi, 2 * (layer * NB + i) + g + 1)
                    nc.vector.tensor_tensor(act_lo[:, ks, rows],
                                            turn[use % 2][:].rearrange("p (k s) -> p k s", k=4),
                                            act_hi[:, ks, rows].bitcast(F32),
                                            ALU.subtract).then_inc(turn_free, 1)

            def forget_logits(layer, h):
                cols = slice(h * HALF, (h + 1) * HALF)
                z, minus = forget[0][:, cols], forget[1][:, cols]
                b = score[h]
                dve.wait_ge(f_done, 2 * layer + h + 1)
                nc.vector.tensor_scalar(z, b[FSPLIT:FSPLIT + FOX_HEADS, :],
                                        bf_c[:, layer:layer + 1], None,
                                        ALU.add).then_inc(c_step, 1)
                dve.wait_ge(c_step, layer * N_C + 2 * h + 1)
                nc.vector.tensor_tensor(z, b[0:FOX_HEADS, :], z, ALU.add).then_inc(c_step, 1)
                dve.wait_ge(c_step, layer * N_C + 2 * h + 2)
                nc.vector.scalar_tensor_tensor(minus, z, -1.0, z, ALU.mult,
                                               ALU.min).then_inc(z_ready, 1)

            def forget_logs(layer):
                dve.wait_ge(e_ready, 2 * (layer + 1))
                nc.vector.scalar_tensor_tensor(forget[0], forget[0], 0.0, forget[1], ALU.min,
                                               ALU.subtract).then_inc(c_step, 1)

            def rotate(layer, kind, t, h):
                n = rotations.index((layer, kind, t, h))
                cols = slice(h * HALF, (h + 1) * HALF)
                b = proj[plan.fill[layer, kind, t, h] % 2]
                dve.wait_ge(proj_done, filled(layer, kind, t, h))
                dve.wait_ge(posb_loaded, layer * N_POSB + 16)
                if kind == "K" and h == 0 and layer:
                    dve.wait_ge(turn_done, plan.use["O", layer - 1, 2 * KT - 1] + 1)
                if n:
                    dve.wait_ge(proj_free, filled(*rotations[n - 1]))
                dve.wait_ge(rope_swapped, n + 1)
                nc.vector.tensor_tensor(rope[:, 0], b[:], posb[:, 0, cols],
                                        ALU.mult).then_inc(rope_mul, 1)
                if t == 0:
                    nc.vector.tensor_tensor(rope[:, 1], rope[:, 1], posb[:, 1, cols],
                                            ALU.mult).then_inc(rope_mul, 1)
                    dve.wait_ge(rope_mul, 2 * (n + 1))
                    nc.vector.tensor_tensor(rope[:, 0], rope[:, 0], rope[:, 1],
                                            ALU.add).then_inc(rope_sum, 1)

            def split_half(layer, kind, t, h):
                cols = slice(h * HALF, (h + 1) * HALF)
                if t < SWA_TILES:
                    src = rope[:, 0]
                else:
                    src = proj[plan.fill[layer, kind, t, h] % 2][:]
                dve.wait_ge(kq_hi, kq_rank[layer, kind, t, h] + 1)
                for head, own in enumerate(HEAD_ROWS):
                    if kind == "Q":
                        lo = nc.vector.scalar_tensor_tensor(
                            q_both[HEAD_ROWS[1 - head], t % 2, head, cols], src[own], SCALE,
                            q_both[own, t % 2, head, cols].bitcast(F32), ALU.mult, ALU.subtract)
                    else:
                        lo = nc.vector.tensor_tensor(k_lo[own, cols], src[own],
                                                     k_hi[own, head, cols].bitcast(F32), ALU.subtract)
                lo.then_inc(proj_free, 1)

            def gate_half(layer, t, h):
                dve.wait_ge(tanh_done, 2 * (layer * TILES + t) + h + 1)
                dst = gate_place(t, h)
                nc.vector.scalar_tensor_tensor(dst, dst, 1.0, proj[plan.fill[layer, "G", t, h] % 2][:],
                                               ALU.add, ALU.mult).then_inc(proj_free, 1)

            def gate_heads(layer, t, h):
                dve.wait_ge(proj_free, filled(layer, "G", t, h))
                dve.wait_ge(o_summed, (layer * TILES + t) * SLOTS + 4 * (h + 1))
                dst = mixed[:, t, h * HALF:(h + 1) * HALF]
                nc.vector.scalar_tensor_tensor(dst, gate_place(t, h), 0.5, dst, ALU.mult,
                                               ALU.mult).then_inc(gated, 1)

            def stage_values(layer, t, h):
                dve.wait_ge(proj_done, filled(layer, "V", t, h))
                if h:
                    dve.wait_ge(turn_done, plan.use["V", layer, t, 0] + 1)
                elif t or layer:
                    dve.wait_ge(gated, gate_order(layer, t, 0))
                nc.vector.tensor_copy(stage[:], proj[plan.fill[layer, "V", t, h] % 2][:]).then_inc(
                    proj_free, 1)

            def stage_outputs(layer, j):
                dve.wait_ge(proj_done, filled(layer, "O", j))
                if j >= 2:
                    dve.wait_ge(turn_done, plan.use["O", layer, j - 2] + 1)
                elif j == 0:
                    dve.wait_ge(proj_free, filled(layer, "Q", SWA_TILES - 1, 1))
                nc.vector.tensor_copy(rope[:, j % 2],
                                      proj[plan.fill[layer, "O", j, 0] % 2][:]).then_inc(proj_free, 1)

            def out_rows(layer, j):
                use = plan.use["O", layer, j]
                half, c = divmod(j, KT)
                dve.wait_ge(turn_done, use + 1)
                dve.wait_ge(y_ready, split_rank(layer, 4 * half + 3, c // 4) + 1)
                dve.wait_ge(out_squared, 2 * KT * layer + j + 1)
                dve.wait_ge(post_loaded, 16 * (layer + 1))
                gains = gain_post[:, c * P:(c + 1) * P].rearrange("p (o d) -> p o d", o=1)
                nc.vector.tensor_tensor(mixed[:, 4 * half:4 * half + 4, c * P:(c + 1) * P],
                                        turn[use % 2][:].rearrange("p (s d) -> p s d", s=4),
                                        gains.broadcast_to([P, 4, P]), ALU.mult
                                        ).then_inc(turn_free, 1)

            def fills_done(layer, t, slot):
                for kind, tt, h in finished_fills(t, slot):
                    if kind == "G":
                        gate_half(layer, tt, h)
                    elif kind == "Q" and tt >= SWA_TILES:
                        split_half(layer, kind, tt, h)

            def value_lo(layer, t, h):
                b = turn[plan.use["V", layer, t, h] % 2][:].rearrange("p (s d) -> p s d", s=4)
                kbs = slice(4 * h, 4 * h + 4)
                dve.wait_ge(v_hi, 2 * values_of(layer, t) + h + 1)
                nc.vector.tensor_tensor(v_sb[:, kbs, HEAD:2 * HEAD], b[:, :, 0:HEAD],
                                        v_sb[:, kbs, 0:HEAD].bitcast(F32), ALU.subtract)
                nc.vector.tensor_tensor(v_sb[:, kbs, 2 * HEAD:3 * HEAD], b[:, :, HEAD:P],
                                        v_sb[:, kbs, 3 * HEAD:4 * HEAD].bitcast(F32),
                                        ALU.subtract).then_inc(turn_free, 1)

            def bias_scores(u, i0, i1):
                if u.slot == 0 and i0 == 0:
                    if u.fox:
                        dve.wait_ge(posb_loaded,
                                    u.layer * N_POSB + 16 + 32 * (u.tile - SWA_TILES + 1))
                    elif u.tile == 0 and u.layer:
                        for i in range(4):
                            dve.wait_ge(x_stored[i], 16 * 2 * u.layer)
                if u.place >= SETS and i0 == 0:
                    dve.wait_ge(turn_done, last_turn[u.index - SETS])
                for a, j in u.chunk_order[i0:i1]:
                    s = u.set_slot(a)
                    index, c0, n = u.score_chunks[a][j]
                    dve.wait_ge(score_done, index + 1)
                    w0 = 2 * P - u.width(a)
                    bias = posb[:, u.head, c0:c0 + n] if u.fox else window[:, w0:w0 + n]
                    nc.vector.tensor_tensor_reduce(prob[:, s, c0:c0 + n], score[index % 2][:, 0:n],
                                                   bias, 1.0, -3e38, ALU.subtract, ALU.max,
                                                   peak[:, s, j:j + 1]).then_inc(score_free, 1)

            def row_maxima(u):
                if not u.fox:
                    s, h = u.set_slot(0), head_of(u.tile, u.head)
                    dve.wait_ge(score_free, u.score_chunks[1][-1][0] + 1)
                    nc.vector.tensor_scalar(nmax[:, s:s + 2], peak[:, s:s + 2, 0],
                                            sink_c[:, u.layer, h:h + 1], -1.0, ALU.max,
                                            ALU.mult).then_inc(nmax_ready, 2)
                    return
                for a in range(2):
                    s = u.set_slot(a)
                    dve.wait_ge(score_free, u.score_chunks[a][-1][0] + 1)
                    if len(u.score_chunks[a]) > 1:
                        args = (peak[:, s, 1:2], -1.0, ALU.max, ALU.mult)
                    else:
                        args = (-1.0, None, ALU.mult)
                    nc.vector.tensor_scalar(nmax[:, s:s + 1], peak[:, s, 0:1],
                                            *args).then_inc(nmax_ready, 1)

            def probs_lo(u, i0, i1):
                for step in u.steps[i0:i1]:
                    dve.wait_ge(pt_hi_done, step.index + 1)
                    s = step.index % 2
                    nc.vector.tensor_tensor(pt_lo[:, s, 0:step.width],
                                            turn[step.use % 2][:, 0:step.width],
                                            pt_hi[:, s, 0:step.width].bitcast(F32),
                                            ALU.subtract).then_inc(turn_free, 1)

            def denominators(u):
                if not u.fox:
                    s, count = u.set_slot(0), (u.layer * SWA_TILES + u.tile) * SLOTS + u.slot + 1
                    dve.wait_ge(exp_done, 2 * u.index + 2)
                    dve.wait_ge(sink_done, 2 * count)
                    nc.vector.tensor_tensor(rsum[:, s:s + 2], rsum[:, s:s + 2], esink[:, s:s + 2],
                                            ALU.add).then_inc(den_ready, 1)
                    dve.wait_ge(den_ready, count)
                    nc.vector.reciprocal(rden[:, s:s + 2], rsum[:, s:s + 2]).then_inc(rden_ready, 2)
                    return
                for a in range(2):
                    s = u.set_slot(a)
                    dve.wait_ge(exp_done, 2 * u.index + a + 1)
                    nc.vector.reciprocal(rden[:, s:s + 1], rsum[:, s:s + 1]).then_inc(rden_ready, 1)

            def normalise(u):
                for a in range(u.fox, 2):
                    s = u.set_slot(a)
                    dve.wait_ge(rden_ready, 2 * u.index + a + 1)
                    row = prob[:, s, 0:u.width(a)]
                    nc.vector.tensor_scalar(row, row, rden[:, s:s + 1], None,
                                            ALU.mult).then_inc(prob_ready, 1)

            def sum_output(u):
                if u.tile == TILES - 2 and u.slot == 0:
                    dve.wait_ge(c_stored, 16 * (u.layer + 1))
                dve.wait_ge(o_copied, u.index + 1)
                nc.vector.tensor_tensor(mixed[u.rows, u.tile, 2 * P * u.m:2 * P * (u.m + 1)],
                                        mix[u.index % 2][u.rows, 0:2 * P],
                                        o_tmp[u.rows], ALU.add).then_inc(o_summed, 1)
                if u.slot % 4 == 3:
                    gate_heads(u.layer, u.tile, u.m // 2)

            def mixed_lo(layer, t, h):
                cols = slice(h * HALF, (h + 1) * HALF)
                dve.wait_ge(y_hi_done, split_rank(layer, t, h) + 1)
                nc.vector.tensor_tensor(act_lo[:, t, cols], mixed[:, t, cols],
                                        act_hi[:, t, cols].bitcast(F32),
                                        ALU.subtract).then_inc(y_ready, 1)

            outputs = []

            def finish_late(layer, t, slot):
                if slot:
                    for kind, tt, h in finished_fills(t, slot - 1):
                        if kind == "Q" and tt < SWA_TILES:
                            rotate(layer, kind, tt, h)
                    fills_done(layer, t, slot - 1)
                    if slot > 1:
                        for kind, tt, h in finished_fills(t, slot - 2):
                            if kind == "Q" and tt < SWA_TILES:
                                split_half(layer, kind, tt, h)
                elif t and not (t in range(SWA_TILES, TILES) and not outputs):
                    fills_done(layer, t - 1, SLOTS - 1)
                if outputs:
                    sum_output(outputs.pop(0))

            for layer in range(DEPTH):
                more = layer + 1 < DEPTH
                if layer == 0:
                    mean_squares(0, 0)
                    norm_rows(0, 0)
                    norm_lo(0, 0)
                    mean_squares(0, 2)
                    norm_rows(0, 2)
                    norm_lo(0, 1)
                    norm_lo(0, 2)
                    norm_lo(0, 3)
                    for i in (4, 6):
                        mean_squares(0, i)
                        norm_rows(0, i)
                else:
                    add_rows(layer - 1, 4)
                    add_rows(layer - 1, 6)
                    mean_squares(layer, 4)
                    norm_rows(layer, 4)
                    mean_squares(layer, 6)
                    norm_rows(layer, 6)
                norm_lo(layer, 4)
                rotate(layer, "K", 0, 0)
                norm_lo(layer, 5)
                norm_lo(layer, 6)
                split_half(layer, "K", 0, 0)
                norm_lo(layer, 7)
                rotate(layer, "Q", 0, 0)
                split_half(layer, "Q", 0, 0)
                forget_logits(layer, 0)
                if layer == 0:
                    set_masks()
                rotate(layer, "K", 0, 1)
                split_half(layer, "K", 0, 1)
                forget_logits(layer, 1)
                stage_values(layer, 0, 0)
                forget_logs(layer)
                rotate(layer, "Q", 0, 1)
                split_half(layer, "Q", 0, 1)
                value_lo(layer, 0, 0)
                stage_values(layer, 0, 1)
                pending = []
                for t in range(TILES):
                    if t >= SWA_TILES:
                        for h in range(2):
                            u = pending.pop(0)
                            probs_lo(u, 0, 2)
                            if h == 0:
                                denominators(pending[0])
                                normalise(pending[0])
                                finish_late(layer, t, 0)
                            probs_lo(u, 2, 4)
                            split_half(layer, "K", t, h)
                            sum_output(u)
                        stage_values(layer, t, 0)
                        value_lo(layer, t, 0)
                        stage_values(layer, t, 1)
                    for slot in range(SLOTS):
                        u = plan.units[layer, t, slot]
                        old = pending.pop(0) if len(pending) == 2 else None
                        if old:
                            probs_lo(old, 0, 2)
                        bias_scores(u, 0, 2)
                        if slot == 0 and plan.use.get(("V", layer, t, 1)):
                            value_lo(layer, t, 1)
                        if pending:
                            denominators(pending[-1])
                        if old:
                            probs_lo(old, 2, 3)
                        bias_scores(u, 2, 3)
                        if pending:
                            normalise(pending[-1])
                        if old:
                            probs_lo(old, 3, 4)
                        bias_scores(u, 3, 4)
                        row_maxima(u)
                        finish_late(layer, t, slot)
                        if t == TILES - 1:
                            for ts, h in split_slots(slot):
                                mixed_lo(layer, ts, h)
                        if (t, slot) == (TILES - 1, SLOTS - 1):
                            stage_outputs(layer, 0)
                        if old:
                            outputs.append(old)
                        pending.append(u)
                probs_lo(pending[0], 0, 2)
                denominators(pending[1])
                normalise(pending[1])
                finish_late(layer, TILES, 0)
                probs_lo(pending[0], 2, 4)
                stage_outputs(layer, 1)
                sum_output(pending[0])
                probs_lo(pending[1], 0, 4)
                sum_output(pending[1])
                stage_outputs(layer, 2)
                out_rows(layer, 0)
                for ts, h in SPLIT_AT[2]:
                    mixed_lo(layer, ts, h)
                out_rows(layer, 1)
                for j in range(3, 2 * KT):
                    for ts, h in SPLIT_AT.get(j, []):
                        mixed_lo(layer, ts, h)
                    out_rows(layer, j - 1)
                    if j == KT:
                        out_mean_squares(layer, 0)
                    if more and j in NORM_TURN_AT:
                        norm_lo(layer + 1, NORM_TURN_AT[j])
                    stage_outputs(layer, j)
                    if j in ADD_AT:
                        add_rows(layer, ADD_AT[j])
                    if j in NORM_AT and more:
                        mean_squares(layer + 1, NORM_AT[j])
                        norm_rows(layer + 1, NORM_AT[j])
                out_rows(layer, 2 * KT - 1)
                out_mean_squares(layer, 1)
            for i in (4, 6):
                add_rows(DEPTH - 1, i)


def w_in_columns():
    swa, kv, fox = SWA_HEADS * HEAD, SWA_KV * HEAD, FOX_HEADS * HEAD
    starts = np.cumsum([0, swa, kv, kv, swa, fox, fox, fox, FOX_HEADS])
    qa, ka, va, ga, qb, kb, vb, fb, gb = (int(s) for s in starts)

    def pair(base, a, b):
        return [base + HEAD * n + d for n in (a, b) for d in range(HEAD)]

    cols = []
    for kind, t in CHUNKS:
        if kind == "O":
            continue
        if t < SWA_TILES:
            base, heads = {"Q": (qa, (t, t + SWA_TILES)), "G": (ga, (t, t + SWA_TILES)),
                           "K": (ka, (0, 1)), "V": (va, (0, 1))}[kind]
        else:
            j = 2 * (t - SWA_TILES)
            base, heads = {"Q": qb, "K": kb, "V": vb, "G": gb}[kind], (j, j + 1)
        cols.append(pair(base, *heads))
    return cols, fb


def lay_out(w_in, w_out):
    cols, fb = w_in_columns()
    w = w_in.reshape(DEPTH, KT, P, -1)
    chunks = [w[..., c].transpose(0, 2, 1, 3) for c in cols]
    swa_rows = [HEAD * n + d for t in range(SWA_TILES) for n in (t, t + SWA_TILES) for d in range(HEAD)]
    rows = swa_rows + list(range(SWA_HEADS * HEAD, D_MODEL))
    wo = w_out[:, rows].reshape(DEPTH, KT, P, KT, P)
    chunks += 2 * [wo[:, :, :, c].transpose(0, 2, 1, 3) for c in range(KT)]
    gates = w[..., fb:fb + FOX_HEADS].transpose(0, 2, 1, 3)
    return np.ascontiguousarray(np.stack(chunks, axis=1)), np.ascontiguousarray(gates)


def constants():
    half = HEAD // 2
    freq = np.float32(10000.0) ** (-np.arange(half, dtype=np.float32) / np.float32(half))
    ang = np.arange(SEQ, dtype=np.float32)[:, None] * freq[None, :]
    cos, sin = np.cos(ang).T, np.sin(ang).T
    rotary = np.stack([np.concatenate([cos] * 4), np.concatenate([-sin, sin] * 2)], axis=1)
    q, k = np.arange(P)[:, None], np.arange(2 * P)[None, :]
    qc, kc = q // CHUNK, k // CHUNK - 2
    return {
        "rotary": rotary.astype(np.float32),
        "ident": np.eye(P, dtype=np.float32),
        "causal": np.where(k[:, :P] <= q, 0.0, -MASKED).astype(np.float32),
        "window": np.where((kc <= qc) & (kc > qc - 2), 0.0, MASKED).astype(np.float32),
    }


def kernel(x, w_in, b_f, sinks, w_out, g_pre, g_post):
    import concourse.bacc as bacc
    from concourse.bass_utils import run_bass_kernel_spmd

    nc = bacc.Bacc("TRN2", target_bir_lowering=False, num_devices=1)
    w_chunks, w_gates = lay_out(np.asarray(w_in), np.asarray(w_out))
    c = constants()
    arrays = {"x_in": np.ascontiguousarray(np.asarray(x)[0]), "w_chunks": w_chunks, "w_gates": w_gates,
              "b_f_in": np.ascontiguousarray(np.asarray(b_f).T), "sinks_in": np.ascontiguousarray(sinks),
              "g_pre_in": np.ascontiguousarray(g_pre), "g_post_in": np.ascontiguousarray(g_post),
              "rotary_in": c["rotary"], "ident_in": c["ident"],
              "causal_in": c["causal"], "window_in": c["window"]}
    args = [nc.dram_tensor(name, a.shape, mybir.dt.from_np(a.dtype), kind="ExternalInput").ap()
            for name, a in arrays.items()]
    out = nc.dram_tensor("rows_out", (SEQ, D_MODEL), F32, kind="ExternalOutput").ap()
    hybrid_trunk(nc, *args, out)
    r = run_bass_kernel_spmd(nc, [arrays], core_ids=[0])
    return r.results[0]["rows_out"][None]
```
